# Optimizing a Trainium2 kernel written in Bass

```python
import math
import jax, jax.numpy as jnp
from jax import lax
import numpy as np

D_MODEL = 4096
BATCH = 1
SEQ = 256
DEPTH = 2

HEAD_DIM = 128
GRID_W = 64
Q_BLOCK = 128
NORM_EPS = 1e-6
NEG_INF = -1e30
A_HEADS = 16
A_KV_HEADS = 4
ROPE_THETA = 10000.0
B_HEADS = 16
NA_ROWS_MAX = 8
NA_COLS = 16
C_HEADS = 32
C_KV_HEADS = 8
C_WINDOW = 128

A_Q = A_HEADS * HEAD_DIM
A_KV = A_KV_HEADS * HEAD_DIM
B_W = B_HEADS * HEAD_DIM
AB_WIDTH = A_Q + B_W
AB_IN = A_Q + 2 * A_KV + 3 * B_W + AB_WIDTH
C_Q = C_HEADS * HEAD_DIM
C_KV = C_KV_HEADS * HEAD_DIM
C_IN = C_Q + 2 * C_KV + C_Q
N_EVEN = (DEPTH + 1) // 2
N_ODD = DEPTH // 2

kernel_name = "hybrid_gqa_natten_swa_gated_encoder"

def rms_norm(x, w):
    xf = x.astype(jnp.float32)
    y = xf * lax.rsqrt(jnp.mean(xf * xf, axis=-1, keepdims=True) + NORM_EPS)
    return (y * w.astype(jnp.float32)).astype(x.dtype)

def split_cols(z, sizes):
    idx = list(np.cumsum(sizes)[:-1])
    return jnp.split(z, idx, axis=-1)

def axial_rope(x, pos):
    half = HEAD_DIM // 2
    quarter = half // 2
    inv = jnp.exp(-math.log(ROPE_THETA) * jnp.arange(0, half, 2, dtype=jnp.float32) / half)
    rows = (pos // GRID_W).astype(jnp.float32)
    cols = (pos % GRID_W).astype(jnp.float32)

    def rot(xh, p):
        ang = p[:, None] * inv[None, :]
        cos = jnp.cos(ang)[None, :, None, :]
        sin = jnp.sin(ang)[None, :, None, :]
        xf = xh.astype(jnp.float32)
        x1, x2 = xf[..., :quarter], xf[..., quarter:]
        return jnp.concatenate([x1 * cos - x2 * sin, x2 * cos + x1 * sin], axis=-1)

    out = jnp.concatenate([rot(x[..., :half], rows), rot(x[..., half:], cols)], axis=-1)
    return out.astype(x.dtype)

def global_gqa(q, k, v):
    B, S, Hq, D = q.shape
    Hkv = k.shape[2]
    G = Hq // Hkv
    nb = S // Q_BLOCK
    scale = D ** -0.5
    qb = q.reshape(B, nb, Q_BLOCK, Hkv, G, D).transpose(1, 0, 2, 3, 4, 5)

    def one(qblk):
        s = jnp.einsum('bqkgd,bskd->bkgqs', qblk, k, preferred_element_type=jnp.float32) * scale
        p = jax.nn.softmax(s, axis=-1).astype(v.dtype)
        return jnp.einsum('bkgqs,bskd->bqkgd', p, v)

    o = lax.map(one, qb)
    return o.transpose(1, 0, 2, 3, 4, 5).reshape(B, S, Hq * D)

def neighbourhood_attention(q, k, v, rpb):
    B, S, H, D = q.shape
    rows = S // GRID_W
    wr = min(NA_ROWS_MAX, rows)
    wc = NA_COLS
    nb = S // Q_BLOCK
    scale = D ** -0.5
    qb = q.reshape(B, nb, Q_BLOCK, H, D).transpose(1, 0, 2, 3, 4)
    r_off = jnp.arange(wr, dtype=jnp.int32)
    c_off = jnp.arange(wc, dtype=jnp.int32)

    def one(args):
        blk, qblk = args
        t = blk * Q_BLOCK + jnp.arange(Q_BLOCK, dtype=jnp.int32)
        r = t // GRID_W
        c = t % GRID_W
        rs = jnp.clip(r - wr // 2, 0, rows - wr)
        cs = jnp.clip(c - wc // 2, 0, GRID_W - wc)
        kr = rs[:, None] + r_off[None, :]
        kc = cs[:, None] + c_off[None, :]
        idx = (kr[:, :, None] * GRID_W + kc[:, None, :]).reshape(Q_BLOCK, wr * wc)
        kg = k[:, idx]
        vg = v[:, idx]
        dr = kr - r[:, None] + (NA_ROWS_MAX - 1)
        dc = kc - c[:, None] + (NA_COLS - 1)
        bias = rpb[:, dr[:, :, None], dc[:, None, :]].reshape(H, Q_BLOCK, wr * wc)
        s = jnp.einsum('bqhd,bqnhd->bhqn', qblk, kg, preferred_element_type=jnp.float32) * scale
        s = s + bias.astype(jnp.float32)[None]
        p = jax.nn.softmax(s, axis=-1).astype(v.dtype)
        return jnp.einsum('bhqn,bqnhd->bqhd', p, vg)

    o = lax.map(one, (jnp.arange(nb, dtype=jnp.int32), qb))
    return o.transpose(1, 0, 2, 3, 4).reshape(B, S, H * D)

def alibi_slopes(n):
    return jnp.exp2(-8.0 * jnp.arange(1, n + 1, dtype=jnp.float32) / n)

def window_gqa_sink(q, k, v, sink):
    B, S, Hq, D = q.shape
    Hkv = k.shape[2]
    G = Hq // Hkv
    nb = S // Q_BLOCK
    W = C_WINDOW
    span = Q_BLOCK + 2 * W
    scale = D ** -0.5
    kp = jnp.pad(k, ((0, 0), (W, W), (0, 0), (0, 0)))
    vp = jnp.pad(v, ((0, 0), (W, W), (0, 0), (0, 0)))
    qb = q.reshape(B, nb, Q_BLOCK, Hkv, G, D).transpose(1, 0, 2, 3, 4, 5)
    slopes = alibi_slopes(Hq).reshape(Hkv, G)
    sink_g = sink.astype(jnp.float32).reshape(Hkv, G)

    def one(args):
        blk, qblk = args
        start = blk * Q_BLOCK
        kb = lax.dynamic_slice_in_dim(kp, start, span, axis=1)
        vb = lax.dynamic_slice_in_dim(vp, start, span, axis=1)
        t = start + jnp.arange(Q_BLOCK, dtype=jnp.int32)
        s_pos = start - W + jnp.arange(span, dtype=jnp.int32)
        dist = jnp.abs(t[:, None] - s_pos[None, :])
        valid = (dist <= W) & (s_pos >= 0)[None, :] & (s_pos < S)[None, :]
        sc = jnp.einsum('bqkgd,bskd->bkgqs', qblk, kb, preferred_element_type=jnp.float32) * scale
        sc = sc - slopes[None, :, :, None, None] * dist.astype(jnp.float32)[None, None, None]
        sc = jnp.where(valid[None, None, None], sc, NEG_INF)
        sink_col = jnp.broadcast_to(sink_g[None, :, :, None, None], (B, Hkv, G, Q_BLOCK, 1))
        p = jax.nn.softmax(jnp.concatenate([sc, sink_col], axis=-1), axis=-1)[..., :span]
        return jnp.einsum('bkgqs,bskd->bqkgd', p.astype(v.dtype), vb)

    o = lax.map(one, (jnp.arange(nb, dtype=jnp.int32), qb))
    return o.transpose(1, 0, 2, 3, 4, 5).reshape(B, S, Hq * D)

def setup_inputs(seed: int = 0) -> dict:
    key = jax.random.key(seed)
    ks = jax.random.split(key, 12)
    f32 = jnp.float32
    x = jax.random.normal(ks[0], (BATCH, SEQ, D_MODEL), f32)
    norm_w = 1.0 + 0.02 * jax.random.normal(ks[1], (DEPTH, D_MODEL), f32)
    w_in_ab = jax.random.normal(ks[2], (N_EVEN, D_MODEL, AB_IN), f32) * D_MODEL ** -0.5
    w_out_ab = jax.random.normal(ks[3], (N_EVEN, AB_WIDTH, D_MODEL), f32) * AB_WIDTH ** -0.5
    q_norm_a = 1.0 + 0.02 * jax.random.normal(ks[4], (N_EVEN, HEAD_DIM), f32)
    k_norm_a = 1.0 + 0.02 * jax.random.normal(ks[5], (N_EVEN, HEAD_DIM), f32)
    rpb_b = 0.1 * jax.random.normal(ks[6], (N_EVEN, B_HEADS, 2 * NA_ROWS_MAX - 1, 2 * NA_COLS - 1), f32)
    w_in_c = jax.random.normal(ks[7], (N_ODD, D_MODEL, C_IN), f32) * D_MODEL ** -0.5
    w_out_c = jax.random.normal(ks[8], (N_ODD, C_Q, D_MODEL), f32) * C_Q ** -0.5
    sink_c = 0.5 * jax.random.normal(ks[9], (N_ODD, C_HEADS), f32)
    final_norm_w = 1.0 + 0.02 * jax.random.normal(ks[10], (D_MODEL,), f32)
    return {"x": x, "norm_w": norm_w, "w_in_ab": w_in_ab, "w_out_ab": w_out_ab,
            "q_norm_a": q_norm_a, "k_norm_a": k_norm_a, "rpb_b": rpb_b,
            "w_in_c": w_in_c, "w_out_c": w_out_c, "sink_c": sink_c,
            "final_norm_w": final_norm_w}

def reference(x, norm_w, w_in_ab, w_out_ab, q_norm_a, k_norm_a, rpb_b, w_in_c, w_out_c, sink_c, final_norm_w):
    B, S, _ = x.shape
    pos = jnp.arange(S, dtype=jnp.int32)
    for layer in range(DEPTH):
        h = rms_norm(x, norm_w[layer])
        if layer % 2 == 0:
            e = layer // 2
            z = h @ w_in_ab[e]
            qa, ka, va, qb, kb, vb, gate = split_cols(z, [A_Q, A_KV, A_KV, B_W, B_W, B_W, AB_WIDTH])
            qa = qa.reshape(B, S, A_HEADS, HEAD_DIM)
            ka = ka.reshape(B, S, A_KV_HEADS, HEAD_DIM)
            va = va.reshape(B, S, A_KV_HEADS, HEAD_DIM)
            qa = axial_rope(rms_norm(qa, q_norm_a[e]), pos)
            ka = axial_rope(rms_norm(ka, k_norm_a[e]), pos)
            oa = global_gqa(qa, ka, va)
            ob = neighbourhood_attention(qb.reshape(B, S, B_HEADS, HEAD_DIM),
                                         kb.reshape(B, S, B_HEADS, HEAD_DIM),
                                         vb.reshape(B, S, B_HEADS, HEAD_DIM), rpb_b[e])
            y = jnp.concatenate([oa, ob], axis=-1) * jax.nn.silu(gate)
            x = x + y @ w_out_ab[e]
        else:
            o = layer // 2
            z = h @ w_in_c[o]
            qc, kc, vc, gate = split_cols(z, [C_Q, C_KV, C_KV, C_Q])
            oc = window_gqa_sink(qc.reshape(B, S, C_HEADS, HEAD_DIM),
                                 kc.reshape(B, S, C_KV_HEADS, HEAD_DIM),
                                 vc.reshape(B, S, C_KV_HEADS, HEAD_DIM), sink_c[o])
            x = x + (oc * jax.nn.silu(gate)) @ w_out_c[o]
    return rms_norm(x, final_norm_w)


_drawn_inputs = setup_inputs


def setup_inputs(seed=0):
    import zlib

    import numpy as np

    out = dict(_drawn_inputs(seed))
    spreads = {}
    factors = {'norm_w': 8.0,
     'q_norm_a': 8.0,
     'k_norm_a': 8.0,
     'rpb_b': 7.11,
     'sink_c': 5.417,
     'final_norm_w': 2.852}
    for name, (base, spread) in spreads.items():
        noise = np.random.default_rng([zlib.crc32(name.encode()), seed]).standard_normal(out[name].shape)
        drawn = base * np.exp(spread * noise) if base else spread * noise
        out[name] = __import__('jax').numpy.asarray(drawn.astype(out[name].dtype))
    for name, factor in factors.items():
        out[name] = (out[name] * factor).astype(out[name].dtype)
    return out
```

```python
from contextlib import ExitStack

import numpy as np

import concourse.bass as bass
from concourse import mybir

ALU = mybir.AluOpType
ACT = mybir.ActivationFunctionType
AX_X = mybir.AxisListType.X
F32 = mybir.dt.float32
F32R = mybir.dt.float32r

P = 128
SEQ = 256
TT = SEQ // P
DM = 4096
KC = DM // P
HD = 128
GRP = 512
HB = GRP // HD
EPS = 1e-6
SCALE = float(HD) ** -0.5
NEG = -1e30
GRID_W = 64
ROWS = SEQ // GRID_W
A_HEADS, A_KV_HEADS, B_HEADS, C_HEADS, C_KV_HEADS = 16, 4, 16, 32, 8
C_WINDOW = 128
NA_COLS, NA_ROWS_MAX = 16, 8

A_Q = 0
A_K = A_HEADS * HD
A_V = A_K + A_KV_HEADS * HD
B_Q = A_V + A_KV_HEADS * HD
B_K = B_Q + B_HEADS * HD
B_V = B_K + B_HEADS * HD
AB_GATE = B_V + B_HEADS * HD
C_Q = 0
C_K = C_HEADS * HD
C_V = C_K + C_KV_HEADS * HD
C_GATE = C_V + C_KV_HEADS * HD

NB = KC
LATE = 2
EARLY = KC // 2 - LATE
BLOCKS = ([(0, c) for c in range(EARLY)] + [(1, c) for c in range(EARLY)]
          + [(0, EARLY + c) for c in range(LATE)] + [(1, EARLY + c) for c in range(LATE)])
DONE0 = BLOCKS.index((0, KC // 2 - 1)) + 1
RING = 4
AHEAD = 2

Q_ROUNDS = (3, 4)
BQ_ROUNDS, BK_ROUNDS = (1, 2), (3, 4)
HEAD_STEP, HEAD_GAP = 5, 5
TO_PT, TO_PV, TO_YT = 3, 4, 6
H_STEPS = (2, 4, 6, 8)
DRAIN0 = DONE0


def head_at(b, offset):
    i, rest = divmod(b - offset - HEAD_STEP, HEAD_GAP)
    return i if rest == 0 and 0 <= i < HB else None


class Pair:

    def __init__(self, w, cols, out, side, before, batch=None, x_batch=None, kv=None):
        self.w, self.cols, self.out, self.side, self.before = w, cols, out, side, before
        self.batch0, self.x_batch0, self.kv = batch, x_batch, kv
        self.x_uses = {"none": 0, "k_norm": 2, "k": 2, "A": 2, "B": 0, "C": 2, "qk": 4, "h": 4}[side]

    def at(self, i):
        self.i = i
        self.n = self.n0 + self.n_step * i
        self.x0 = self.x00 + self.x_step * i
        if self.batch0 is not None:
            self.batch = self.batch0 + i
        return self


def plan():
    g = GRP
    out_cols = lambda p0: ((2 * g * p0, 2 * g), (2 * g * p0 + g, 2 * g))
    a = lambda j: ((A_Q + g * j, g), (AB_GATE + g * j, g))
    qk = lambda j: ((B_Q + g * j, g), (B_K + g * j, g))
    vg = lambda j: ((B_V + g * j, g), (AB_GATE + A_HEADS * HD + g * j, g))
    c = lambda j: ((C_Q + g * j, g), (C_GATE + g * j, g))
    kvc = lambda j: ((C_K + g * j, g), (C_V + g * j, g))
    loops = [
        (1, [Pair("in_ab", ((A_K, 0), (A_V, 0)), "kv", "none", None)]),
        (1, [Pair("in_ab", a(0), "qg", "k_norm", "kv")]),
        (3, [Pair("in_ab", a(1), "qg", "A", "qg", batch=0)]),
        (1, [Pair("in_ab", qk(0), "qk", "A", "qg", batch=3)]),
        (1, [Pair("in_ab", vg(0), "vg", "qk", "qk")]),
        (3, [Pair("in_ab", qk(1), "qk", "B", "vg", batch=4), Pair("in_ab", vg(1), "vg", "qk", "qk")]),
        (1, [Pair("out_ab", out_cols(0), "x1", "B", "vg", batch=7)]),
        (3, [Pair("out_ab", out_cols(1), "x1", "h", "x1", x_batch=0)]),
        (1, [Pair("in_c", kvc(0), "kv", "h", "x1", x_batch=3)]),
        (1, [Pair("in_c", c(0), "qg", "k", "kv")]),
        (3, [Pair("in_c", c(1), "qg", "C", "qg", batch=8)]),
        (1, [Pair("in_c", kvc(1), "kv", "C", "qg", batch=11)]),
        (1, [Pair("in_c", c(4), "qg", "k", "kv")]),
        (3, [Pair("in_c", c(5), "qg", "C", "qg", batch=12)]),
        (1, [Pair("out_c", out_cols(0), "x2", "C", "qg", batch=15)]),
        (2, [Pair("out_c", out_cols(1), "x2", "none", "x2")]),
        (1, [Pair("out_c", out_cols(3), "x2", "none", "x2")]),
    ]
    n = x = 0
    for rounds, pairs in loops:
        x_step = sum(p.x_uses for p in pairs)
        at_x = x
        for k, p in enumerate(pairs):
            p.n0, p.n_step, p.x00, p.x_step = n + k, len(pairs), at_x, x_step
            p.last = False
            at_x += p.x_uses
        n += rounds * len(pairs)
        x += rounds * x_step
    loops[-1][1][0].last = True
    return loops


PLAN = plan()
ATTN_PAIRS = {p.batch0: p for _, pairs in PLAN for p in pairs if p.batch0 is not None}
H_FIRST_X = next(p.x00 for _, pairs in PLAN for p in pairs if p.side == "h")
X1_FIRST = next(p.n0 for _, pairs in PLAN for p in pairs if p.out == "x1")
X2_FIRST = next(p.n0 for _, pairs in PLAN for p in pairs if p.out == "x2")
PAIRS_ALL = sum(rounds * len(pairs) for rounds, pairs in PLAN)


def walk(eng, body):
    for rounds, pairs in PLAN:
        if rounds == 1:
            for p in pairs:
                body(p.at(0))
        else:
            with eng.Fori(0, rounds) as i:
                for p in pairs:
                    body(p.at(i))


def ahead(p, b):
    if p.last and b + AHEAD >= NB:
        return None
    return p.n * NB + b + AHEAD, (b + AHEAD) % RING


def maxima_after(kind, h):
    return 2 * (h + 1) if kind in "AB" else 3 * (h + 1) - 32


def inverses_after(kind, h):
    return h + 1 if kind in "AB" else 2 * (h + 1) - 32


def build(nc, x, w_in_ab, w_out_ab, w_in_c, w_out_c, norm_cols, q_norm, k_norm, final_w, bias_b, sinks,
          ident_c, cos_c, sin_c, neg_dist_c, slopes_c, out):
    weights = {"in_ab": w_in_ab, "out_ab": w_out_ab, "in_c": w_in_c, "out_c": w_out_c}
    x_rows = x.rearrange("(t p) n -> p t n", p=P)
    out_rows = out.rearrange("(t p) n -> p t n", p=P)
    x1_dram = nc.dram_tensor("x1_residual", [SEQ, DM], F32, kind="Internal").ap()
    x1_rows = x1_dram.rearrange("(t p) n -> p t n", p=P)

    with ExitStack() as ctx:
        arena_bytes = 212 * 1024 - 5120
        arena = ctx.enter_context(nc.sbuf_tensor("arena", [P, arena_bytes], mybir.dt.uint8))
        base = (nc.sbuf_base - arena_bytes + 31) // 32 * 32
        top = [base]

        def place(name, shape, dt, at=None):
            size = int(np.prod(shape[1:])) * 4
            where = top[0] if at is None else at
            if at is None:
                top[0] += (size + 31) // 32 * 32
                assert top[0] <= base + arena_bytes - 32, (name, top[0] - base)
            return nc.alloc_sbuf_tensor_at(name, shape, dt, offset=where), where

        h_hi, h_at = place("h_hi", [P, KC, SEQ], F32R)
        h_lo, _ = place("h_lo", [P, KC, SEQ], F32R)
        y_hi, y_at = place("y_hi", [P, KC, SEQ], F32R)
        y_lo, _ = place("y_lo", [P, KC, SEQ], F32R)
        raw, _ = place("raw", [P, RING, 2, GRP], F32)
        w_hi, _ = place("w_hi", [P, RING, 2, GRP], F32R)
        w_lo, _ = place("w_lo", [P, RING, 2, GRP], F32R)
        za, _ = place("za", [P, TT, GRP], F32)
        zb, _ = place("zb", [P, TT, GRP], F32)
        qT, q_at = place("qT", [P, HB, SEQ], F32)
        kT, _ = place("kT", [P, HB, SEQ], F32)
        v, _ = place("v", [P, TT, GRP], F32)
        probs, e_at = place("probs", [P, TT, SEQ], F32)
        probsT, _ = place("probsT", [P, TT, SEQ], F32)
        y, _ = place("y", [P, TT, HD], F32)
        table, t_at = place("table", [P, 4, TT, HD], F32)
        ident, _ = place("ident", [P, P], F32)
        norm_w, _ = place("norm_w", [P, 2, KC], F32)
        sink, _ = place("sink", [P, C_HEADS], F32)
        neg_sink, _ = place("neg_sink", [P, C_HEADS], F32)
        slope, _ = place("slope", [P, C_HEADS], F32)
        sq_cols, _ = place("sq_cols", [P, TT, 8], F32)
        sq_sum, _ = place("sq_sum", [P, TT], F32)
        sq_part, _ = place("sq_part", [P, TT], F32)
        var, _ = place("var", [P, TT * HB], F32)
        minus_half, _ = place("minus_half", [P, TT * HB], F32)
        rms, _ = place("rms", [P, TT], F32)
        neg_rms, _ = place("neg_rms", [P, TT], F32)
        head_rms, _ = place("head_rms", [P, TT * HB], F32)
        q_scale, _ = place("q_scale", [P, TT * HB], F32)
        neg_max, _ = place("neg_max", [P, TT], F32)
        exp_bias, _ = place("exp_bias", [P, TT], F32)
        sums, _ = place("sums", [P, TT], F32)
        sink_term, _ = place("sink_term", [P, TT], F32)
        total, _ = place("total", [P, TT], F32)
        inv_sum, _ = place("inv_sum", [P, TT], F32)
        x_in, _ = place("x_in", [P, TT, DM], F32, at=y_at)
        x_fin, _ = place("x_fin", [P, TT, DM], F32, at=h_at)
        fin_w, _ = place("fin_w", [P, DM], F32, at=h_at + TT * DM * 4)
        gate_exp, _ = place("gate_exp", [P, TT, GRP], F32, at=e_at)
        swap, _ = place("swap", [P, TT, GRP], F32, at=q_at)
        norm_bc, _ = place("norm_bc", [P, 2, HD], F32, at=e_at)
        bias, _ = place("bias", [P, 2, TT, SEQ], F32, at=t_at)
        dist, _ = place("dist", [P, TT, SEQ], F32, at=t_at)
        cos_q, sin_q, cos_k, sin_k = (table[:, k] for k in range(4))

        proj = [[ctx.enter_context(nc.psum_tensor(f"proj{g}{t}", [P, GRP], F32)) for t in range(TT)]
                for g in range(2)]
        sc_ps = ctx.enter_context(nc.psum_tensor("sc_ps", [P, TT, SEQ], F32))
        tr_ps = ctx.enter_context(nc.psum_tensor("tr_ps", [P, TT, SEQ], F32))
        o_ps = ctx.enter_context(nc.psum_tensor("o_ps", [P, TT, HD * 2], F32))
        x_ps = ctx.enter_context(nc.psum_tensor("x_ps", [P, 2, SEQ], F32))
        first_ps = [x_ps, sc_ps, tr_ps, o_ps]

        def sem(name):
            return ctx.enter_context(nc.semaphore(name))

        x_loaded = [sem(f"x_loaded{k}") for k in range(4)]
        consts_loaded = sem("consts_loaded")
        tables_loaded = sem("tables_loaded")
        raw_loaded = [sem(f"raw_loaded{k}") for k in range(RING)]
        bias_loaded = [sem("bias_loaded0"), sem("bias_loaded1")]
        dist_loaded = sem("dist_loaded")
        res_loaded = [sem("res_loaded0"), sem("res_loaded1")]
        x1_stored = [sem("x1_stored0"), sem("x1_stored1")]
        fin_loaded = sem("fin_loaded")
        out_stored = sem("out_stored")
        hi_ready = sem("hi_ready")
        lo_ready = sem("lo_ready")
        block_done = sem("block_done")
        drained = [sem("drained0"), sem("drained1")]
        first_filled = sem("first_filled")
        first_hi = sem("first_hi")
        first_split = sem("first_split")
        squared = sem("squared")
        tables_made = sem("tables_made")
        minus_half_set = sem("minus_half_set")
        var_ready = sem("var_ready")
        pow_done = sem("pow_done")
        neg_rms_ready = sem("neg_rms_ready")
        neg_sink_ready = sem("neg_sink_ready")
        var_steps = sem("var_steps")
        roped = sem("roped")
        x_filled = sem("x_filled")
        x_hi = sem("x_hi")
        x_drained = sem("x_drained")
        gated = sem("gated")
        scored = sem("scored")
        maxima = sem("maxima")
        probs_ready = sem("probs_ready")
        inverses = sem("inverses")
        tr_filled = sem("tr_filled")
        tr_drained = sem("tr_drained")
        y_hi_ready = sem("y_hi_ready")
        pv_done = sem("pv_done")
        y_ready = sem("y_ready")
        summed = sem("summed")
        x2_steps = sem("x2_steps")
        scaled = sem("scaled")
        scaled_act = sem("scaled_act")

        TABLE_STEPS, ROPE_STEPS, VAR0_STEPS = 8, 9, 2
        N_CONSTS = 16 * 4

        block = ctx.enter_context(nc.Block())

        @block.sync
        def _(sp):
            quarter = DM // 4
            for k in range(4):
                cols = slice(k * quarter, (k + 1) * quarter)
                sp.dma_start(x_in[:, :, cols], x_rows[:, :, cols]).then_inc(x_loaded[k], 16)
                if k == 0:
                    sp.dma_start(ident[:], ident_c).then_inc(consts_loaded, 16)
                    sp.dma_start(norm_w[:], norm_cols).then_inc(consts_loaded, 16)
                    sp.dma_start(sink[:], sinks.partition_broadcast(P)).then_inc(consts_loaded, 16)
                    sp.dma_start(slope[:], slopes_c).then_inc(consts_loaded, 16)

            def load_tables():
                for k, src in enumerate((cos_c, sin_c, cos_c, sin_c)):
                    sp.dma_start(table[:, k], src).then_inc(tables_loaded, 16)
                sp.dma_start(norm_bc[:, 0], q_norm.partition_broadcast(P)).then_inc(tables_loaded, 16)
                sp.dma_start(norm_bc[:, 1], k_norm.partition_broadcast(P)).then_inc(tables_loaded, 16)

            def load_bias(p, i):
                head = (p.batch - 4) * HB + i
                if p.batch0 == 4 and i < 2:
                    sp.wait_ge(roped, 5 * ROPE_STEPS)
                if not (p.batch0 == 4 and i < 2 and isinstance(p.i, int)):
                    sp.wait_ge(maxima, maxima_after("B", p.batch * HB + i - 2))
                src = bias_b[bass.ds(head, 1)].rearrange("a (t p) k -> p (a t) k", p=P)
                sp.dma_start(bias[:, i % 2], src).then_inc(bias_loaded[i % 2], 16)

            def body(p):
                w = weights[p.w]
                for b, (g, c) in enumerate(BLOCKS):
                    if isinstance(p.n, int) and p.n * NB + b < RING:
                        pass
                    else:
                        sp.wait_ge(lo_ready, p.n * NB + b - RING + 1)
                    col, step = p.cols[g]
                    src = w[c * 2 * P:(c + 1) * 2 * P, bass.ds(col + step * p.i, GRP)]
                    sp.dma_start(raw[:, b % RING], src.rearrange("(j p) n -> p j n", p=P)) \
                        .then_inc(raw_loaded[b % RING], 16)
                    if p.n0 == 0 and b == 8:
                        load_tables()
                    if p.side == "B" and b in (2, 7, 12, 17):
                        load_bias(p, (b - 2) // 5)
                    if p.side == "h" and p.batch0 is None:
                        if b in (8, 10):
                            k = (b - 8) // 2
                            sp.wait_ge(drained[k], 2 * p.n)
                            first = (p.x_batch0 + p.i) * 2 * GRP + k * GRP
                            sp.dma_start(x1_rows[:, :, bass.ds(first, GRP)], (za, zb)[k][:]) \
                                .then_inc(x1_stored[k], 16)
                        if b in (14, 18) and p.out == "x1":
                            k = (b - 14) // 4
                            if k == 0:
                                sp.wait_ge(x1_stored[0], 16 * (p.n - X1_FIRST))
                                sp.wait_ge(x_drained, p.x0 + 2)
                            else:
                                sp.wait_ge(x_drained, p.x0 + 4)
                                sp.wait_ge(x1_stored[1], 16 * (p.n - X1_FIRST))
                            sp.dma_start((za, zb)[k][:], x_rows[:, :, bass.ds(p.cols[k][0] + p.cols[k][1] * p.i, GRP)]) \
                                .then_inc(res_loaded[k], 16)
                    if p.n0 == X1_FIRST and b in (10, 28):
                        k = (b - 10) // 18
                        sp.wait_ge(*((x_filled, p.x0) if k == 0 else (y_ready, 8 * HB)))
                        sp.dma_start((za, zb)[k][:], x_rows[:, :, k * GRP:(k + 1) * GRP]).then_inc(res_loaded[k], 16)
                    if p.side == "k" and p.batch0 is None and p.n0 == ATTN_PAIRS[8].n0 - 1 and b == 10:
                        sp.wait_ge(maxima, maxima_after("B", 2 * A_HEADS - 1))
                        sp.dma_start(dist[:], neg_dist_c).then_inc(dist_loaded, 16)
                    if p.n0 == X2_FIRST and b == 12:
                        sp.wait_ge(block_done, X2_FIRST * NB)
                        sp.wait_ge(x1_stored[0], 16 * 4)
                        sp.wait_ge(x1_stored[1], 16 * 4)
                        sp.dma_start(x_fin[:], x1_rows).then_inc(fin_loaded, 16)
                        sp.dma_start(fin_w[:], final_w.partition_broadcast(P)).then_inc(fin_loaded, 16)

            walk(sp, body)
            for k in range(4):
                cols = slice(k * quarter, (k + 1) * quarter)
                sp.wait_ge(scaled, k + 1)
                sp.dma_start(out_rows[:, 0, cols], x_fin[:, 0, cols]).then_inc(out_stored, 16)
                sp.wait_ge(scaled_act, k + 1)
                sp.dma_start(out_rows[:, 1, cols], x_fin[:, 1, cols]).then_inc(out_stored, 16)
            sp.wait_ge(out_stored, 16 * 8)

        @block.gpsimd
        def _(pool):
            nc.gpsimd.memset(minus_half[:], -0.5).then_inc(minus_half_set, 1)
            pool.wait_ge(minus_half_set, 1)
            for n, (dst, cols) in enumerate([(rms, TT)] + [(head_rms, TT * HB)] * 5 + [(rms, TT)] * 2):
                pool.wait_ge(var_ready, n + 1)
                nc.gpsimd.tensor_tensor(dst[:, 0:cols], var[:, 0:cols], minus_half[:, 0:cols], ALU.pow) \
                    .then_inc(pow_done, 1)

        @block.scalar
        def _(act):
            def split_hi(n, slot):
                if not (isinstance(n, int) and n < RING):
                    act.wait_ge(block_done, n - RING + 1)
                act.wait_ge(raw_loaded[slot], 16 * loads(n, slot))
                nc.scalar.activation(w_hi[:, slot], raw[:, slot], ACT.Copy).then_inc(hi_ready, 1)

            def loads(n, slot):
                return (n - slot) // RING + 1 if isinstance(n, int) else None

            def split_hi_at(p, b):
                m = ahead(p, b)
                if m is None:
                    return
                n, slot = m
                if not (isinstance(n, int) and n < RING):
                    act.wait_ge(block_done, n - RING + 1)
                act.wait_ge(raw_loaded[slot], 16 * (p.n * (NB // RING) + (b + AHEAD) // RING + 1))
                nc.scalar.activation(w_hi[:, slot], raw[:, slot], ACT.Copy).then_inc(hi_ready, 1)
                act.wait_ge(hi_ready, n + 1)

            def drain(p, g, out, n):
                for t in range(TT):
                    src = proj[g][t]
                    if g == 0:
                        dst = v if out == "vg" else za
                    else:
                        dst = v if out == "kv" else zb
                    if t == 0:
                        act.wait_ge(block_done, n * NB + (DONE0 if g == 0 else NB))
                    gate = g == 1 and out in ("qg", "vg")
                    last = nc.scalar.activation(dst[:, t], src[:], ACT.Copy, scale=rms[:, t:t + 1])
                    if gate:
                        last = nc.scalar.activation(gate_exp[:, t], src[:], ACT.Exp, scale=neg_rms[:, t:t + 1])
                    last.then_inc(drained[g], 1)

            act.wait_ge(consts_loaded, N_CONSTS)
            for m in range(KC // 2):
                act.wait_ge(first_filled, m + 1)
                for j in range(2):
                    k = 2 * m + j
                    last = nc.scalar.activation(h_hi[:, k], first_ps[m % 4][:, j], ACT.Copy, scale=norm_w[:, 0, k:k + 1])
                last.then_inc(first_hi, 1)
            for n in range(AHEAD):
                split_hi(n, n)

            def body(p):
                for b in range(NB):
                    split_hi_at(p, b)
                    if b == 0 and p.before not in (None, "x1", "x2"):
                        drain(p, 1, p.before, p.n - 1)
                    if b == DRAIN0 and p.out not in ("x1", "x2"):
                        if p.n0 == 0:
                            act.wait_ge(neg_rms_ready, 1)
                        if p.n0 == X1_FIRST + 4:
                            act.wait_ge(neg_rms_ready, 2)
                            act.wait_ge(x1_stored[0], 16 * 4)
                            act.wait_ge(x1_stored[1], 16 * 4)
                            act.wait_ge(summed, 4 * 4 + 1)
                        drain(p, 0, p.out, p.n)
                    if p.side in ("A", "C", "k", "k_norm"):
                        for k, step in enumerate(Q_ROUNDS):
                            if b == step:
                                act.wait_ge(x_filled, p.x0 + k + 1)
                                dst = kT if p.side in ("k", "k_norm") else qT
                                nc.scalar.activation(dst[:, 2 * k:2 * k + 2], x_ps[:], ACT.Copy).then_inc(x_drained, 1)
                    if p.side == "qk":
                        for k, step in enumerate(BQ_ROUNDS + BK_ROUNDS):
                            if b == step:
                                act.wait_ge(x_filled, p.x0 + k + 1)
                                dst, i = (qT, k) if k < 2 else (kT, k - 2)
                                nc.scalar.activation(dst[:, 2 * i:2 * i + 2], x_ps[:], ACT.Copy).then_inc(x_drained, 1)
                    if p.side == "h" and b in H_STEPS:
                        m = H_STEPS.index(b)
                        act.wait_ge(x_filled, p.x0 + m + 1)
                        for j in range(2):
                            k = (p.x_batch0 + p.i) * 8 + 2 * m + j
                            last = nc.scalar.activation(h_hi[:, bass.ds(k, 1)].rearrange("p a n -> p (a n)"), x_ps[:, j],
                                                        ACT.Copy, scale=norm_w[:, 1, bass.ds(k, 1)])
                        last.then_inc(x_hi, 1)
                    if p.side in ("A", "B", "C"):
                        attend(p, b)

            def attend(p, b):
                i = head_at(b, 1)
                if i is not None:
                    h = p.batch * HB + i
                    if i == 0:
                        act.wait_ge(gated, 3 * (p.batch + 1))
                    act.wait_ge(maxima, maxima_after(p.side, h))
                    for t in range(TT):
                        scale = {"A": q_scale[:, t * HB + i:t * HB + i + 1], "B": 1.0, "C": SCALE}[p.side]
                        last = nc.scalar.activation(probs[:, t], sc_ps[:, t], ACT.Exp, bias=exp_bias[:, t:t + 1],
                                                    scale=scale, accum_out=sums[:, t:t + 1])
                    if p.side == "C":
                        last = nc.scalar.activation(sink_term[:], exp_bias[:], ACT.Exp, bias=sink[:, bass.ds(h - 32, 1)])
                    last.then_inc(probs_ready, 1)
                i = head_at(b, TO_PT)
                if i is not None:
                    h = p.batch * HB + i
                    act.wait_ge(tr_filled, 2 * h + 1)
                    nc.scalar.activation(probsT[:], tr_ps[:], ACT.Copy).then_inc(tr_drained, 1)
                i = head_at(b, TO_YT + 1)
                if i is not None:
                    h = p.batch * HB + i
                    row = (p.batch - (8 if p.side == "C" else 0)) * HB + i
                    act.wait_ge(tr_filled, 2 * h + 2)
                    nc.scalar.activation(y_hi[:, bass.ds(row, 1)].rearrange("p a n -> p (a n)"), tr_ps[:, 0], ACT.Copy) \
                        .then_inc(y_hi_ready, 1)

            walk(act, body)
            act.wait_ge(pow_done, 8)
            act.wait_ge(x2_steps, 4 * 8)
            for k in range(4):
                cols = slice(k * DM // 4, (k + 1) * DM // 4)
                nc.scalar.activation(x_fin[:, 1, cols], x_fin[:, 1, cols], ACT.Copy, scale=rms[:, 1:2]) \
                    .then_inc(scaled_act, 1)

        @block.vector
        def _(dve):
            def split_lo(p, b):
                m = ahead(p, b)
                if m is None:
                    return
                n, slot = m
                dve.wait_ge(hi_ready, n + 1)
                nc.vector.tensor_tensor(w_lo[:, slot], raw[:, slot], w_hi[:, slot].bitcast(F32), ALU.subtract) \
                    .then_inc(lo_ready, 1)
                dve.wait_ge(lo_ready, n + 1)

            dve.wait_ge(consts_loaded, N_CONSTS)
            for m in range(KC // 2):
                dve.wait_ge(first_hi, m + 1)
                for j in range(2):
                    k = 2 * m + j
                    last = nc.vector.scalar_tensor_tensor(h_lo[:, k], first_ps[m % 4][:, j], norm_w[:, 0, k:k + 1],
                                                          h_hi[:, k].bitcast(F32), ALU.mult, ALU.subtract)
                last.then_inc(first_split, 1)
            for n in range(AHEAD):
                dve.wait_ge(hi_ready, n + 1)
                nc.vector.tensor_tensor(w_lo[:, n], raw[:, n], w_hi[:, n].bitcast(F32), ALU.subtract).then_inc(lo_ready, 1)

            def first_squares(b):
                if 2 <= b < 10:
                    m = b - 2
                    cols = slice(m * GRP, (m + 1) * GRP)
                    for t in range(TT):
                        last = nc.vector.tensor_tensor_reduce(swap[:, t], x_in[:, t, cols], x_in[:, t, cols], 1.0, 0.0,
                                                              ALU.mult, ALU.add, sq_cols[:, t, m:m + 1])
                    last.then_inc(squared, 1)
                if b == 10:
                    dve.wait_ge(squared, 8)
                    nc.vector.tensor_reduce(sq_sum[:], sq_cols[:], AX_X, ALU.add).then_inc(squared, 1)
                    dve.wait_ge(squared, 9)
                    nc.vector.tensor_scalar(var[:, 0:TT], sq_sum[:], 1.0 / DM, EPS, ALU.mult, ALU.add).then_inc(var_ready, 1)
                if b == 12:
                    dve.wait_ge(pow_done, 1)
                    nc.vector.tensor_scalar(neg_rms[:], rms[:], -1.0, None, ALU.mult).then_inc(neg_rms_ready, 1)
                    nc.vector.tensor_scalar(neg_sink[:], sink[:], -1.0, None, ALU.mult).then_inc(neg_sink_ready, 1)
                    nc.vector.memset(sq_sum[:], 0.0).then_inc(summed, 1)
                if b == 20:
                    dve.wait_ge(tables_loaded, 16 * 6)
                    halves = lambda ap: ap.rearrange("p (h q e) -> p h q e", h=2, q=2)
                    for cos, sin, w in ((cos_q, sin_q, norm_bc[:, 0]), (cos_k, sin_k, norm_bc[:, 1])):
                        for t in range(TT):
                            nc.vector.tensor_tensor(cos[:, t], cos[:, t], w, ALU.mult).then_inc(tables_made, 1)
                            for q in range(2):
                                s = halves(sin[:, t])[:, :, q]
                                last = nc.vector.tensor_tensor(s, s, halves(w)[:, :, 1 - q], ALU.mult)
                            last.then_inc(tables_made, 1)

            def rope(b, cos, sin, k, for_k):
                s = k * ROPE_STEPS
                heads = za[:].rearrange("p t (h d) -> p (t h) d", d=HD)
                if b == 0:
                    dve.wait_ge(tables_made, TABLE_STEPS)
                    nc.vector.tensor_tensor(swap[:], za[:], za[:], ALU.mult).then_inc(roped, 1)
                    dve.wait_ge(roped, s + 1)
                    nc.vector.tensor_reduce(q_scale[:], swap[:].rearrange("p t (h d) -> p (t h) d", d=HD), AX_X, ALU.add) \
                        .then_inc(roped, 1)
                    dve.wait_ge(roped, s + 2)
                    nc.vector.tensor_scalar(var[:], q_scale[:], 1.0 / HD, EPS, ALU.mult, ALU.add).then_inc(var_ready, 1)
                if b == 1:
                    quarters = lambda ap: ap.rearrange("p (h f q e) -> p (h f) q e", h=HB, f=2, q=2)
                    for t in range(TT):
                        for q in range(2):
                            sines = sin[:, t].rearrange("p (f q e) -> p f q e", f=2, q=2)[:, :, q]
                            nc.vector.tensor_tensor(
                                swap[:, t].rearrange("p (h f q e) -> p h f q e", h=HB, f=2, q=2)[:, :, :, q],
                                za[:, t].rearrange("p (h f q e) -> p h f q e", h=HB, f=2, q=2)[:, :, :, 1 - q],
                                sines.unsqueeze(1).to_broadcast([P, HB, 2, HD // 4]), ALU.mult).then_inc(roped, 1)
                if b == 2:
                    dve.wait_ge(roped, s + 6)
                    for t in range(TT):
                        last = nc.vector.tensor_tensor(za[:, t].rearrange("p (h d) -> p h d", h=HB),
                                                       za[:, t].rearrange("p (h d) -> p h d", h=HB),
                                                       cos[:, t].unsqueeze(1).to_broadcast([P, HB, HD]), ALU.mult)
                    last.then_inc(roped, 1)
                    dve.wait_ge(roped, s + 7)
                    nc.vector.tensor_tensor(za[:], za[:], swap[:], ALU.add).then_inc(roped, 1)
                    dve.wait_ge(pow_done, k + 2)
                    dve.wait_ge(roped, s + 8)
                    if for_k:
                        nc.vector.tensor_tensor(heads, heads, head_rms[:].unsqueeze(2).to_broadcast([P, TT * HB, HD]),
                                                ALU.mult).then_inc(roped, 1)
                    else:
                        nc.vector.tensor_scalar(q_scale[:], head_rms[:], SCALE, None, ALU.mult).then_inc(roped, 1)

            def gate(p, b):
                s = 3 * p.batch
                if b == 1:
                    dve.wait_ge(drained[1], 2 * p.n)
                    nc.vector.tensor_scalar(gate_exp[:], gate_exp[:], 1.0, None, ALU.add).then_inc(gated, 1)
                if b == 3:
                    dve.wait_ge(gated, s + 1)
                    nc.vector.reciprocal(gate_exp[:], gate_exp[:]).then_inc(gated, 1)
                if b == 4:
                    dve.wait_ge(gated, s + 2)
                    nc.vector.tensor_tensor(zb[:], zb[:], gate_exp[:], ALU.mult).then_inc(gated, 1)

            def attend(p, b):
                i = head_at(b, 1)
                if i is not None:
                    h = p.batch * HB + i
                    m = maxima_after(p.side, h - 1)
                    dve.wait_ge(scored, h + 1)
                    if p.side == "B":
                        if i < 2:
                            dve.wait_ge(bias_loaded[i], 32 * (p.batch - 4) + 16)
                        else:
                            dve.wait_ge(bias_loaded[i - 2], 32 * (p.batch - 4) + 32)
                        nc.vector.scalar_tensor_tensor(sc_ps[:], sc_ps[:], SCALE, bias[:, i % 2], ALU.mult, ALU.add) \
                            .then_inc(maxima, 1)
                        dve.wait_ge(maxima, m + 1)
                    if p.side == "C":
                        nc.vector.scalar_tensor_tensor(sc_ps[:], dist[:], slope[:, bass.ds(h - 32, 1)], sc_ps[:],
                                                       ALU.mult, ALU.add).then_inc(maxima, 1)
                        dve.wait_ge(maxima, m + 1)
                    dst = exp_bias if p.side == "B" else neg_max
                    nc.vector.tensor_reduce(dst[:], sc_ps[:], AX_X, ALU.max, negate=True).then_inc(maxima, 1)
                    if p.side == "A":
                        dve.wait_ge(maxima, m + 1)
                        scales = q_scale[:].rearrange("p (t h) -> p t h", t=TT)[:, :, i]
                        nc.vector.tensor_tensor(exp_bias[:], neg_max[:], scales, ALU.mult).then_inc(maxima, 1)
                    if p.side == "C":
                        dve.wait_ge(maxima, m + 2)
                        nc.vector.tensor_scalar(exp_bias[:], neg_max[:], SCALE, neg_sink[:, bass.ds(h - 32, 1)],
                                                ALU.mult, ALU.min).then_inc(maxima, 1)
                i = head_at(b, 2)
                if i is not None:
                    h = p.batch * HB + i
                    dve.wait_ge(probs_ready, h + 1)
                    if p.side == "C":
                        nc.vector.tensor_tensor(total[:], sums[:], sink_term[:], ALU.add).then_inc(inverses, 1)
                        dve.wait_ge(inverses, inverses_after("C", h) - 1)
                    nc.vector.reciprocal(inv_sum[:], (total if p.side == "C" else sums)[:]).then_inc(inverses, 1)
                i = head_at(b, TO_PV + 1)
                if i is not None:
                    h = p.batch * HB + i
                    dve.wait_ge(pv_done, h + 1)
                    dve.wait_ge(inverses, inverses_after(p.side, h))
                    if i == 0:
                        dve.wait_ge(gated, 3 * (p.batch + 1))
                    for t in range(TT):
                        last = nc.vector.scalar_tensor_tensor(y[:, t], o_ps[:, t, 0:HD], inv_sum[:, t:t + 1],
                                                              zb[:, t, i * HD:(i + 1) * HD], ALU.mult, ALU.mult)
                    last.then_inc(y_ready, 1)
                i = head_at(b, TO_YT + 1)
                if i is not None:
                    h = p.batch * HB + i
                    row = (p.batch - (8 if p.side == "C" else 0)) * HB + i
                    dve.wait_ge(y_hi_ready, h + 1)
                    nc.vector.tensor_tensor(y_lo[:, bass.ds(row, 1)].rearrange("p a n -> p (a n)"), tr_ps[:, 0],
                                            y_hi[:, bass.ds(row, 1)].rearrange("p a n -> p (a n)").bitcast(F32),
                                            ALU.subtract).then_inc(tr_drained, 1)

            def add_x1(g, n):
                dve.wait_ge(block_done, n * NB + (DONE0 if g == 0 else NB))
                dve.wait_ge(res_loaded[g], 16 * (n - X1_FIRST + 1))
                for t in range(TT):
                    z = (za, zb)[g]
                    nc.vector.tensor_tensor(z[:, t], proj[g][t][:], z[:, t], ALU.add).then_inc(drained[g], 1)

            def square_x1(p, g):
                z = (za, zb)[g]
                s = 4 * (p.n - 1 - X1_FIRST) + 2 * g + 1
                dve.wait_ge(drained[g], 2 * p.n)
                dve.wait_ge(summed, s)
                for t in range(TT):
                    last = nc.vector.tensor_tensor_reduce(swap[:, t], z[:, t], z[:, t], 1.0, 0.0, ALU.mult, ALU.add,
                                                          sq_part[:, t:t + 1])
                last.then_inc(summed, 1)
                dve.wait_ge(summed, s + 1)
                nc.vector.tensor_tensor(sq_sum[:], sq_sum[:], sq_part[:], ALU.add).then_inc(summed, 1)

            def add_x2(p, g, n, groups):
                s = 4 * (2 * (n - X2_FIRST) + g)
                first = groups * GRP
                cols = bass.ds(first, GRP)
                dve.wait_ge(block_done, n * NB + (DONE0 if g == 0 else NB))
                if not isinstance(s, int) or s:
                    dve.wait_ge(x2_steps, s)
                for t in range(TT):
                    nc.vector.tensor_tensor(za[:, t], proj[g][t][:], x_fin[:, t, cols], ALU.add).then_inc(drained[g], 1)
                dve.wait_ge(drained[g], 2 * (n + 1))
                for t in range(TT):
                    last = nc.vector.tensor_tensor_reduce(swap[:, t], za[:, t], za[:, t], 1.0, 0.0, ALU.mult, ALU.add,
                                                          sq_part[:, t:t + 1])
                last.then_inc(x2_steps, 1)
                for t in range(TT):
                    nc.vector.tensor_tensor(x_fin[:, t, cols], za[:, t], fin_w[:, cols], ALU.mult).then_inc(x2_steps, 1)
                dve.wait_ge(x2_steps, s + 1)
                nc.vector.tensor_tensor(sq_sum[:], sq_sum[:], sq_part[:], ALU.add).then_inc(x2_steps, 1)

            def body(p):
                for b in range(NB):
                    split_lo(p, b)
                    if p.n0 == 0:
                        first_squares(b)
                    if b == 0 and p.before == "x1":
                        add_x1(1, p.n - 1)
                    if b == 0 and p.before == "x2":
                        add_x2(p, 1, p.n - 1, (p.n - 1 - X2_FIRST) * 2 + 1)
                    if b == DRAIN0 and p.out == "x1":
                        add_x1(0, p.n)
                    if b == DRAIN0 and p.out == "x2":
                        if p.n0 == X2_FIRST:
                            dve.wait_ge(fin_loaded, 32)
                        add_x2(p, 0, p.n, (p.n - X2_FIRST) * 2)
                    if p.side == "k_norm":
                        if b == 0:
                            dve.wait_ge(drained[0], 2 * p.n)
                        rope(b, cos_k, sin_k, 0, True)
                    if p.side == "A":
                        if b == 0:
                            dve.wait_ge(drained[0], 2 * p.n)
                        rope(b, cos_q, sin_q, p.batch + 1, False)
                    if p.side == "h":
                        if b in (1, 3):
                            square_x1(p, (b - 1) // 2)
                        if b in H_STEPS:
                            m = H_STEPS.index(b)
                            dve.wait_ge(x_hi, 4 * (p.x_batch0 + p.i) + m + 1)
                            for j in range(2):
                                k = (p.x_batch0 + p.i) * 8 + 2 * m + j
                                last = nc.vector.scalar_tensor_tensor(
                                    h_lo[:, bass.ds(k, 1)].rearrange("p a n -> p (a n)"), x_ps[:, j],
                                    norm_w[:, 1, bass.ds(k, 1)],
                                    h_hi[:, bass.ds(k, 1)].rearrange("p a n -> p (a n)").bitcast(F32),
                                    ALU.mult, ALU.subtract)
                            last.then_inc(x_drained, 1)
                        if p.out == "kv" and b == 10:
                            dve.wait_ge(summed, 4 * 4 + 1)
                            nc.vector.tensor_scalar(var[:, 0:TT], sq_sum[:], 1.0 / DM, EPS, ALU.mult, ALU.add) \
                                .then_inc(var_ready, 1)
                        if p.out == "kv" and b == 12:
                            dve.wait_ge(pow_done, 7)
                            nc.vector.tensor_scalar(neg_rms[:], rms[:], -1.0, None, ALU.mult).then_inc(neg_rms_ready, 1)
                            nc.vector.memset(sq_sum[:], 0.0).then_inc(summed, 1)
                    if p.side in ("A", "B", "C"):
                        if p.side == "C" and p.batch0 == 8 and b == 0:
                            dve.wait_ge(dist_loaded, 16)
                        gate(p, b)
                        attend(p, b)

            walk(dve, body)
            add_x2(None, 1, PAIRS_ALL - 1, 7)
            dve.wait_ge(x2_steps, 4 * 8)
            nc.vector.tensor_scalar(var[:, 0:TT], sq_sum[:], 1.0 / DM, EPS, ALU.mult, ALU.add).then_inc(var_ready, 1)
            dve.wait_ge(pow_done, 8)
            for k in range(4):
                cols = slice(k * DM // 4, (k + 1) * DM // 4)
                nc.vector.tensor_scalar(x_fin[:, 0, cols], x_fin[:, 0, cols], rms[:, 0:1], None, ALU.mult) \
                    .then_inc(scaled, 1)

        @block.tensor
        def _(pe):
            pe.wait_ge(consts_loaded, N_CONSTS)
            for m in range(KC // 2):
                if m % 4 == 0:
                    pe.wait_ge(x_loaded[m // 4], 16)
                if m >= 4:
                    pe.wait_ge(first_split, m - 3)
                for j in range(2):
                    for t in range(TT):
                        k = 2 * m + j
                        last = nc.tensor.transpose(first_ps[m % 4][:, j, t * P:(t + 1) * P],
                                                   x_in[:, t, k * P:(k + 1) * P], ident[:])
                last.then_inc(first_filled, 1)

            def product(p, b):
                g, c = BLOCKS[b]
                hi, lo = (y_hi, y_lo) if p.w in ("out_ab", "out_c") else (h_hi, h_lo)
                slot = b % RING
                pe.wait_ge(lo_ready, p.n * NB + b + 1)
                if c == 0 and p.n0 > 0:
                    pe.wait_ge(drained[g], 2 * p.n)
                if p.n0 == 0 and g == 0:
                    pe.wait_ge(first_split, c + 1)
                if p.n0 == X1_FIRST + 4 and g == 0:
                    pe.wait_ge(x_drained, H_FIRST_X + c + 1)
                if p.n0 in (X1_FIRST, X2_FIRST) and g == 0:
                    first = 0 if p.n0 == X1_FIRST else 32
                    pe.wait_ge(tr_drained, 2 * (first + 2 * c + 2))
                for j in range(2):
                    k = 2 * c + j
                    for t in range(TT):
                        toks = slice(t * P, (t + 1) * P)
                        nc.tensor.matmul(proj[g][t][:], hi[:, k, toks], w_hi[:, slot, j], start=(k == 0), stop=False)
                        nc.tensor.matmul(proj[g][t][:], hi[:, k, toks], w_lo[:, slot, j], start=False, stop=False)
                        last = nc.tensor.matmul(proj[g][t][:], lo[:, k, toks], w_hi[:, slot, j], start=False,
                                                stop=(k == KC - 1))
                last.then_inc(block_done, 1)

            def heads_round(p, k, src, i):
                if not (isinstance(p.x0, int) and p.x0 + k == 0):
                    pe.wait_ge(x_drained, p.x0 + k)
                for j in range(2):
                    for t in range(TT):
                        d = (2 * i + j) * HD
                        last = nc.tensor.transpose(x_ps[:, j, t * P:(t + 1) * P], src[:, t, d:d + HD], ident[:])
                last.then_inc(x_filled, 1)

            def attend(p, b):
                kv = {"A": p.batch, "B": None, "C": p.batch - (8 if p.batch0 < 12 else 12)}[p.side]
                i = head_at(b, 0)
                if i is not None:
                    h = p.batch * HB + i
                    if i == 0:
                        pe.wait_ge(x_drained, p.x0 + p.x_uses)
                    if not (isinstance(h, int) and h == 0):
                        pe.wait_ge(probs_ready, h) if p.batch0 > 0 or i > 0 else None
                    k = kT[:, i] if p.side == "B" else kT[:, bass.ds(kv, 1)].rearrange("p a n -> p (a n)")
                    for t in range(TT):
                        last = nc.tensor.matmul(sc_ps[:, t], qT[:, i, t * P:(t + 1) * P], k, start=True, stop=True)
                    last.then_inc(scored, 1)
                i = head_at(b, TO_PT)
                if i is not None:
                    h = p.batch * HB + i
                    pe.wait_ge(probs_ready, h + 1)
                    if p.batch0 > 0 or i > 0:
                        pe.wait_ge(tr_drained, 2 * h)
                    for kt in range(TT):
                        for t in range(TT):
                            last = nc.tensor.transpose(tr_ps[:, kt, t * P:(t + 1) * P],
                                                       probs[:, t, kt * P:(kt + 1) * P], ident[:])
                    last.then_inc(tr_filled, 1)
                i = head_at(b, TO_PV)
                if i is not None:
                    h = p.batch * HB + i
                    pe.wait_ge(tr_drained, 2 * h + 1)
                    for t in range(TT):
                        for kt in range(TT):
                            cols = slice(i * HD, (i + 1) * HD) if p.side == "B" else bass.ds(kv * HD, HD)
                            last = nc.tensor.matmul(o_ps[:, t, 0:HD], probsT[:, kt, t * P:(t + 1) * P], v[:, kt, cols],
                                                    start=(kt == 0), stop=(kt == TT - 1))
                    last.then_inc(pv_done, 1)
                i = head_at(b, TO_YT)
                if i is not None:
                    h = p.batch * HB + i
                    pe.wait_ge(y_ready, h + 1)
                    for t in range(TT):
                        last = nc.tensor.transpose(tr_ps[:, 0, t * P:(t + 1) * P], y[:, t], ident[:])
                    last.then_inc(tr_filled, 1)

            def body(p):
                for b in range(NB):
                    for k, step in enumerate(Q_ROUNDS):
                        if b == step and p.side in ("A", "C", "k", "k_norm"):
                            if k == 0 and p.side in ("A", "k_norm"):
                                n = 0 if p.side == "k_norm" else p.batch + 1
                                pe.wait_ge(roped, ROPE_STEPS * (n + 1))
                            if k == 0 and p.side in ("C", "k"):
                                pe.wait_ge(drained[0], 2 * p.n)
                            heads_round(p, k, za, k)
                    if p.side == "qk":
                        for k, step in enumerate(BQ_ROUNDS + BK_ROUNDS):
                            if b == step:
                                if k in (0, 2):
                                    pe.wait_ge(drained[k // 2], 2 * p.n)
                                heads_round(p, k, za if k < 2 else zb, k % 2)
                    if p.side == "h" and b in H_STEPS:
                        m = H_STEPS.index(b)
                        if m in (0, 2):
                            pe.wait_ge(drained[m // 2], 2 * p.n)
                        heads_round(p, m, (za, zb)[m // 2], m % 2)
                    if p.side in ("A", "B", "C"):
                        attend(p, b)
                    product(p, b)

            walk(pe, body)


def constants():
    pos = np.arange(SEQ)
    half, quarter = HD // 2, HD // 4
    inv = np.exp(-np.log(10000.0) * np.arange(0, half, 2, dtype=np.float64) / half)
    cos = np.zeros((SEQ, HD))
    sin = np.zeros((SEQ, HD))
    for h, coord in enumerate((pos // GRID_W, pos % GRID_W)):
        ang = coord.astype(np.float32)[:, None] * inv.astype(np.float32)[None, :]
        lo = h * half
        cos[:, lo:lo + quarter] = cos[:, lo + quarter:lo + half] = np.cos(ang)
        sin[:, lo:lo + quarter] = -np.sin(ang)
        sin[:, lo + quarter:lo + half] = np.sin(ang)
    tiles = lambda a: np.ascontiguousarray(a.reshape(TT, P, -1).transpose(1, 0, 2).astype(np.float32))
    dist = np.abs(pos[:, None] - pos[None, :])
    neg_dist = np.where(dist <= C_WINDOW, -dist.astype(np.float64), NEG)
    slopes = np.exp2(-8.0 * np.arange(1, C_HEADS + 1) / C_HEADS) / SCALE
    return {
        "ident_c": np.eye(P, dtype=np.float32),
        "cos_c": tiles(cos),
        "sin_c": tiles(sin),
        "neg_dist_c": tiles(neg_dist),
        "slopes_c": np.broadcast_to(slopes.astype(np.float32), (P, C_HEADS)).copy(),
    }


def bias_layout(rpb):
    pos = np.arange(SEQ)
    r, c = pos // GRID_W, pos % GRID_W
    wr = min(NA_ROWS_MAX, ROWS)
    rs = np.clip(r - wr // 2, 0, ROWS - wr)
    cs = np.clip(c - NA_COLS // 2, 0, GRID_W - NA_COLS)
    inside = ((r[None, :] >= rs[:, None]) & (r[None, :] < rs[:, None] + wr)
              & (c[None, :] >= cs[:, None]) & (c[None, :] < cs[:, None] + NA_COLS))
    dr = np.clip(r[None, :] - r[:, None] + NA_ROWS_MAX - 1, 0, 2 * NA_ROWS_MAX - 2)
    dc = np.clip(c[None, :] - c[:, None] + NA_COLS - 1, 0, 2 * NA_COLS - 2)
    return np.where(inside[None], rpb[:, dr, dc], np.float32(NEG))


def kernel(**inputs):
    import concourse.bacc as _bacc
    from concourse.bass_utils import run_bass_kernel_spmd as _run

    a = {k: np.asarray(val) for k, val in inputs.items()}
    arrays = {
        "x": a["x"][0],
        "w_in_ab": a["w_in_ab"][0],
        "w_out_ab": a["w_out_ab"][0],
        "w_in_c": a["w_in_c"][0],
        "w_out_c": a["w_out_c"][0],
        "norm_cols": a["norm_w"].reshape(2, KC, P).transpose(2, 0, 1),
        "q_norm": a["q_norm_a"][0],
        "k_norm": a["k_norm_a"][0],
        "final_w": a["final_norm_w"],
        "bias_b": bias_layout(a["rpb_b"][0]),
        "sinks": a["sink_c"][0],
    }
    arrays.update(constants())
    nc = _bacc.Bacc("TRN2", target_bir_lowering=False, num_devices=1)
    ins, aps = {}, []
    for name, val in arrays.items():
        ins[f"in_{name}"] = np.ascontiguousarray(val)
        aps.append(nc.dram_tensor(f"in_{name}", val.shape, mybir.dt.from_np(val.dtype), kind="ExternalInput").ap())
    out = nc.dram_tensor("out_0", (SEQ, DM), F32, kind="ExternalOutput").ap()
    build(nc, *aps, out)
    r = _run(nc, [ins], core_ids=[0])
    return r.results[0]["out_0"].reshape(1, SEQ, DM)
```

```python
from contextlib import ExitStack

import numpy as np

import concourse.bass as bass
from concourse import mybir

ALU = mybir.AluOpType
ACT = mybir.ActivationFunctionType
AX_X = mybir.AxisListType.X
F32 = mybir.dt.float32
F32R = mybir.dt.float32r

P = 128
SEQ = 256
TT = SEQ // P
DM = 4096
KC = DM // P
HD = 128
GRP = 512
HB = GRP // HD
EPS = 1e-6
SCALE = float(HD) ** -0.5
NEG = -1e30
SWDGE_BYTES = 1024
GRID_W = 64
ROWS = SEQ // GRID_W
A_HEADS, A_KV_HEADS, B_HEADS, C_HEADS, C_KV_HEADS = 16, 4, 16, 32, 8
C_WINDOW = 128
NA_COLS, NA_ROWS_MAX = 16, 8

A_Q = 0
A_K = A_HEADS * HD
A_V = A_K + A_KV_HEADS * HD
B_Q = A_V + A_KV_HEADS * HD
B_K = B_Q + B_HEADS * HD
B_V = B_K + B_HEADS * HD
AB_GATE = B_V + B_HEADS * HD
C_Q = 0
C_K = C_HEADS * HD
C_V = C_K + C_KV_HEADS * HD
C_GATE = C_V + C_KV_HEADS * HD

NB = KC
LATE = 2
EARLY = KC // 2 - LATE
BLOCKS = ([(0, c) for c in range(EARLY)] + [(1, c) for c in range(EARLY)]
          + [(0, EARLY + c) for c in range(LATE)] + [(1, EARLY + c) for c in range(LATE)])
DONE0 = BLOCKS.index((0, KC // 2 - 1)) + 1
RING = 4
AHEAD = 2

Q_ROUNDS = {"A": (5, 6), "C": (3, 4)}
BQ_ROUNDS, BK_ROUNDS = (1, 2), (3, 4)
HEAD_STEP = {"A": 7, "B": 5, "C": 5}
HEAD_GAP = 5
TO_PROBS, TO_PT, TO_GT, TO_PV, TO_Y, TO_REST = 1, 3, 4, 5, 6, 7
H_STEPS = (2, 4, 6, 8)
FIRST_AHEAD = 2
OUT_PIECES = ((0, GRP), (GRP, 2 * GRP), (2 * GRP, 4 * GRP), (4 * GRP, 6 * GRP), (6 * GRP, DM))
DRAIN0 = DONE0


def head_at(p, b, offset):
    i, rest = divmod(b - offset - HEAD_STEP[p.side], HEAD_GAP)
    return i if rest == 0 and 0 <= i < HB else None


class Pair:

    def __init__(self, w, cols, out, side, before, batch=None, x_batch=None, v=None):
        self.w, self.cols, self.out, self.side, self.before = w, cols, out, side, before
        self.batch0, self.x_batch0, self.v0 = batch, x_batch, v
        self.x_uses = {"none": 0, "k_norm": 2, "k": 2, "A": 2, "B": 0, "C": 2, "qk": 4, "h": 4}[side]

    def at(self, i):
        self.i = i
        self.n = self.n0 + self.n_step * i
        self.x0 = self.x00 + self.x_step * i
        if self.batch0 is not None:
            self.batch = self.batch0 + i
        if self.v0 is not None:
            self.v = self.v0 + i
        return self


def plan():
    g = GRP
    out_cols = lambda p0: ((2 * g * p0, 2 * g), (2 * g * p0 + g, 2 * g))
    a = lambda j: ((A_Q + g * j, g), (AB_GATE + g * j, g))
    qk = lambda j: ((B_Q + g * j, g), (B_K + g * j, g))
    vg = lambda j: ((B_V + g * j, g), (AB_GATE + A_HEADS * HD + g * j, g))
    c = lambda j: ((C_Q + g * j, g), (C_GATE + g * j, g))
    kvc = lambda j: ((C_K + g * j, g), (C_V + g * j, g))
    loops = [
        (1, [Pair("in_ab", ((A_K, 0), (A_V, 0)), "kv", "none", None)]),
        (1, [Pair("in_ab", a(0), "qg", "k_norm", "kv", v=0)]),
        (3, [Pair("in_ab", a(1), "qg", "A", "qg", batch=0)]),
        (1, [Pair("in_ab", qk(0), "qk", "A", "qg", batch=3)]),
        (1, [Pair("in_ab", vg(0), "vg", "qk", "qk", v=1)]),
        (3, [Pair("in_ab", qk(1), "qk", "B", "vg", batch=4), Pair("in_ab", vg(1), "vg", "qk", "qk", v=2)]),
        (1, [Pair("out_ab", out_cols(0), "x1", "B", "vg", batch=7)]),
        (3, [Pair("out_ab", out_cols(1), "x1", "h", "x1", x_batch=0)]),
        (1, [Pair("in_c", kvc(0), "kv", "h", "x1", x_batch=3)]),
        (1, [Pair("in_c", c(0), "qg", "k", "kv", v=5)]),
        (3, [Pair("in_c", c(1), "qg", "C", "qg", batch=8)]),
        (1, [Pair("in_c", kvc(1), "kv", "C", "qg", batch=11)]),
        (1, [Pair("in_c", c(4), "qg", "k", "kv", v=6)]),
        (3, [Pair("in_c", c(5), "qg", "C", "qg", batch=12)]),
        (1, [Pair("out_c", out_cols(0), "x2", "C", "qg", batch=15)]),
        (2, [Pair("out_c", out_cols(1), "x2", "none", "x2")]),
        (1, [Pair("out_c", out_cols(3), "x2", "none", "x2")]),
    ]
    n = x = 0
    for rounds, pairs in loops:
        x_step = sum(p.x_uses for p in pairs)
        at_x = x
        for k, p in enumerate(pairs):
            p.n0, p.n_step, p.x00, p.x_step = n + k, len(pairs), at_x, x_step
            p.last = False
            at_x += p.x_uses
        n += rounds * len(pairs)
        x += rounds * x_step
    loops[-1][1][0].last = True
    return loops


PLAN = plan()
ATTN_PAIRS = {p.batch0: p for _, pairs in PLAN for p in pairs if p.batch0 is not None}
H_FIRST_X = next(p.x00 for _, pairs in PLAN for p in pairs if p.side == "h")
X1_FIRST = next(p.n0 for _, pairs in PLAN for p in pairs if p.out == "x1")
X2_FIRST = next(p.n0 for _, pairs in PLAN for p in pairs if p.out == "x2")
PAIRS_ALL = sum(rounds * len(pairs) for rounds, pairs in PLAN)


def walk(eng, body):
    for rounds, pairs in PLAN:
        if rounds == 1:
            for p in pairs:
                body(p.at(0))
        else:
            with eng.Fori(0, rounds) as i:
                for p in pairs:
                    body(p.at(i))


def kv_head(p):
    return {"A": p.batch, "B": None, "C": p.batch - (8 if p.batch0 < 12 else 12)}[p.side]


def rounds_at(p, b):
    if p.side in ("A", "C", "k", "k_norm"):
        to = "q" if p.side in "AC" else "k"
        steps = Q_ROUNDS["A" if p.side in ("A", "k_norm") else "C"]
        return [(n, to, n) for n, step in enumerate(steps) if step == b]
    if p.side == "qk":
        return [(n, "qk"[n // 2], n % 2) for n, step in enumerate(BQ_ROUNDS + BK_ROUNDS) if step == b]
    return []


def ahead(p, b):
    if p.last and b + AHEAD >= NB:
        return None
    return p.n * NB + b + AHEAD, (b + AHEAD) % RING


def maxima_after(kind, h):
    return 2 * (h + 1) if kind in "AB" else 3 * (h + 1) - 32


def inverses_after(kind, h):
    return h + 1 if kind in "AB" else 2 * (h + 1) - 32


def build(nc, x, w_in_ab, w_out_ab, w_in_c, w_out_c, norm_cols, q_norm, k_norm, final_w, bias_b, sinks,
          ident_c, cos_c, sin_c, neg_dist_c, slopes_c, out):
    weights = {"in_ab": w_in_ab, "out_ab": w_out_ab, "in_c": w_in_c, "out_c": w_out_c}
    x_rows = x.rearrange("(t p) n -> p t n", p=P)
    out_rows = out.rearrange("(t p) n -> p t n", p=P)
    x1_dram = nc.dram_tensor("x1_residual", [SEQ, DM], F32, kind="Internal").ap()
    x1_rows = x1_dram.rearrange("(t p) n -> p t n", p=P)

    with ExitStack() as ctx:
        arena_bytes = (nc.sbuf_usable_end - nc.sbuf_base) // 32 * 32 - 32
        arena = ctx.enter_context(nc.sbuf_tensor("arena", [P, arena_bytes], mybir.dt.uint8))
        base = (nc.sbuf_base - arena_bytes + 31) // 32 * 32
        top = [base]

        def place(name, shape, dt, at=None):
            size = int(np.prod(shape[1:])) * 4
            where = top[0] if at is None else at
            if at is None:
                top[0] += (size + 31) // 32 * 32
                assert top[0] <= base + arena_bytes - 32, (name, top[0] - base)
            return nc.alloc_sbuf_tensor_at(name, shape, dt, offset=where), where

        h_hi, h_at = place("h_hi", [P, KC, SEQ], F32R)
        h_lo, _ = place("h_lo", [P, KC, SEQ], F32R)
        y_hi, y_at = place("y_hi", [P, KC, SEQ], F32R)
        y_lo, _ = place("y_lo", [P, KC, SEQ], F32R)
        raw, _ = place("raw", [P, RING, 2, GRP], F32)
        w_hi, _ = place("w_hi", [P, RING, 2, GRP], F32R)
        w_lo, _ = place("w_lo", [P, RING, 2, GRP], F32R)
        za, _ = place("za", [P, TT, GRP], F32)
        zb, _ = place("zb", [P, TT, GRP], F32)
        qT_hi, q_at = place("qT_hi", [P, HB, SEQ], F32R)
        qT_lo, _ = place("qT_lo", [P, HB, SEQ], F32R)
        kT_hi, _ = place("kT_hi", [P, HB, SEQ], F32R)
        kT_lo, _ = place("kT_lo", [P, HB, SEQ], F32R)
        v_hi, _ = place("v_hi", [P, TT, GRP], F32R)
        v_lo, _ = place("v_lo", [P, TT, GRP], F32R)
        pick_hi, _ = place("pick_hi", [P, TT, HD], F32R)
        pick_lo, _ = place("pick_lo", [P, TT, HD], F32R)
        probs, p_at = place("probs", [P, TT, SEQ], F32)
        probsT_hi, _ = place("probsT_hi", [P, TT, SEQ], F32R)
        probsT_lo, _ = place("probsT_lo", [P, TT, SEQ], F32R)
        y, _ = place("y", [P, SEQ], F32)
        table, t_at = place("table", [P, 4, TT, HD], F32)
        ident, _ = place("ident", [P, P], F32)
        norm_w, _ = place("norm_w", [P, 2, KC], F32)
        sink, _ = place("sink", [P, C_HEADS], F32)
        neg_sink, _ = place("neg_sink", [P, C_HEADS], F32)
        slope, _ = place("slope", [P, C_HEADS], F32)
        sq_cols, _ = place("sq_cols", [P, TT, 8], F32)
        sq_sum, _ = place("sq_sum", [P, TT], F32)
        sq_part, _ = place("sq_part", [P, TT], F32)
        var, _ = place("var", [P, TT * HB], F32)
        minus_half, _ = place("minus_half", [P, TT * HB], F32)
        rms, _ = place("rms", [P, TT], F32)
        head_rms, _ = place("head_rms", [P, TT * HB], F32)
        q_scale, _ = place("q_scale", [P, TT * HB], F32)
        neg_max, _ = place("neg_max", [P, TT], F32)
        exp_bias, _ = place("exp_bias", [P, TT], F32)
        sums, _ = place("sums", [P, TT], F32)
        sink_term, _ = place("sink_term", [P, TT], F32)
        total, _ = place("total", [P, TT], F32)
        inv_sum, _ = place("inv_sum", [P, TT], F32)
        warm, _ = place("warm", [P, 1], F32)
        x_in, _ = place("x_in", [P, TT, DM], F32, at=y_at)
        x_fin, _ = place("x_fin", [P, TT, DM], F32, at=h_at)
        fin_w, _ = place("fin_w", [P, DM], F32, at=h_at + TT * DM * 4)
        swap, _ = place("swap", [P, TT, GRP], F32, at=q_at)
        norm_bc, _ = place("norm_bc", [P, 2, HD], F32, at=p_at)
        bias, _ = place("bias", [P, 2, TT, SEQ], F32, at=t_at)
        dist, _ = place("dist", [P, TT, SEQ], F32, at=t_at)
        cos_q, sin_q, cos_k, sin_k = (table[:, k] for k in range(4))

        proj = [[ctx.enter_context(nc.psum_tensor(f"proj{g}{t}", [P, GRP], F32)) for t in range(TT)]
                for g in range(2)]
        sc_ps = ctx.enter_context(nc.psum_tensor("sc_ps", [P, TT, SEQ], F32))
        tr_ps = ctx.enter_context(nc.psum_tensor("tr_ps", [P, TT, SEQ], F32))
        o_ps = ctx.enter_context(nc.psum_tensor("o_ps", [P, TT, SEQ], F32))
        x_ps = ctx.enter_context(nc.psum_tensor("x_ps", [P, 2, SEQ], F32))
        first_ps = [x_ps, sc_ps, tr_ps, o_ps]

        def sem(name):
            return ctx.enter_context(nc.semaphore(name))

        x_loaded = [sem(f"x_loaded{k}") for k in range(DM // GRP)]
        ident_loaded = sem("ident_loaded")
        norm_loaded = sem("norm_loaded")
        tables_loaded = sem("tables_loaded")
        raw_loaded = [sem(f"raw_loaded{k}") for k in range(RING)]
        bias_loaded = [sem("bias_loaded0"), sem("bias_loaded1")]
        dist_loaded = sem("dist_loaded")
        res_loaded = [sem("res_loaded0"), sem("res_loaded1")]
        x1_stored = [sem("x1_stored0"), sem("x1_stored1")]
        fin_loaded = sem("fin_loaded")
        out_stored = sem("out_stored")
        hi_ready = sem("hi_ready")
        lo_ready = sem("lo_ready")
        block_done = sem("block_done")
        last_tile = sem("last_tile")
        drained = [sem("drained0"), sem("drained1")]
        first_filled = sem("first_filled")
        first_hi = sem("first_hi")
        first_split = sem("first_split")
        squared = sem("squared")
        tables_made = sem("tables_made")
        minus_half_set = sem("minus_half_set")
        var_ready = sem("var_ready")
        pow_done = sem("pow_done")
        roped = sem("roped")
        x_filled = sem("x_filled")
        x_hi = sem("x_hi")
        x_drained = sem("x_drained")
        scored = sem("scored")
        maxima = sem("maxima")
        probs_ready = sem("probs_ready")
        inverses = sem("inverses")
        gate_scaled = sem("gate_scaled")
        pt_filled = sem("pt_filled")
        pt_hi_ready = sem("pt_hi_ready")
        pt_split = sem("pt_split")
        gt_filled = sem("gt_filled")
        gt_ready = sem("gt_ready")
        pv_done = sem("pv_done")
        y_made = sem("y_made")
        y_hi_ready = sem("y_hi_ready")
        y_split = sem("y_split")
        v_picked = sem("v_picked")
        v_hi_ready = sem("v_hi_ready")
        summed = sem("summed")
        x2_steps = sem("x2_steps")
        scaled = sem("scaled")
        scaled_act = sem("scaled_act")

        TABLE_STEPS, ROPE_STEPS = 8, 9

        block = ctx.enter_context(nc.Block())

        @block.sync
        def _(sp):
            def load_x(k):
                cols = slice(k * GRP, (k + 1) * GRP)
                sp.dma_start(x_in[:, :, cols], x_rows[:, :, cols]).then_inc(x_loaded[k], 16)

            sp.dma_start(ident[:], ident_c).then_inc(ident_loaded, 16)
            load_x(0)
            sp.dma_start(norm_w[:], norm_cols).then_inc(norm_loaded, 16)

            def load_tables():
                for k, src in enumerate((cos_c, sin_c, cos_c, sin_c)):
                    sp.dma_start(table[:, k], src).then_inc(tables_loaded, 16)
                sp.dma_start(norm_bc[:, 0], q_norm.partition_broadcast(P)).then_inc(tables_loaded, 16)
                sp.dma_start(norm_bc[:, 1], k_norm.partition_broadcast(P)).then_inc(tables_loaded, 16)
                sp.dma_start(sink[:], sinks.partition_broadcast(P)).then_inc(tables_loaded, 16)
                sp.dma_start(slope[:], slopes_c).then_inc(tables_loaded, 16)

            def load_bias(p, i):
                head = (p.batch - 4) * HB + i
                if p.batch0 == 4 and i < 2:
                    sp.wait_ge(roped, 5 * ROPE_STEPS)
                if not (p.batch0 == 4 and i < 2 and isinstance(p.i, int)):
                    sp.wait_ge(maxima, maxima_after("B", p.batch * HB + i - 2))
                src = bias_b[bass.ds(head, 1)].rearrange("a (t p) k -> p (a t) k", p=P)
                sp.dma_start(bias[:, i % 2], src).then_inc(bias_loaded[i % 2], 16)

            def body(p):
                w = weights[p.w]
                for b, (g, c) in enumerate(BLOCKS):
                    if isinstance(p.n, int) and p.n * NB + b < RING:
                        pass
                    else:
                        sp.wait_ge(lo_ready, p.n * NB + b - RING + 1)
                    col, step = p.cols[g]
                    src = w[c * 2 * P:(c + 1) * 2 * P, bass.ds(col + step * p.i, GRP)]
                    sp.dma_start(raw[:, b % RING], src.rearrange("(j p) n -> p j n", p=P)) \
                        .then_inc(raw_loaded[b % RING], 16)
                    if p.n0 == 0 and b % 2 == 0 and b // 2 + 1 < DM // GRP:
                        load_x(b // 2 + 1)
                    if p.n0 == 0 and b == 14:
                        load_tables()
                    if p.side == "B" and b in (2, 7, 12, 17):
                        load_bias(p, (b - 2) // 5)
                    if p.side == "h" and p.batch0 is None:
                        if b in (8, 10):
                            k = (b - 8) // 2
                            sp.wait_ge(drained[k], 2 * p.n)
                            first = (p.x_batch0 + p.i) * 2 * GRP + k * GRP
                            sp.dma_start(x1_rows[:, :, bass.ds(first, GRP)], (za, zb)[k][:]) \
                                .then_inc(x1_stored[k], 16)
                        if b in (14, 18) and p.out == "x1":
                            k = (b - 14) // 4
                            if k == 0:
                                sp.wait_ge(x1_stored[0], 16 * (p.n - X1_FIRST))
                                sp.wait_ge(x_drained, p.x0 + 2)
                            else:
                                sp.wait_ge(x_drained, p.x0 + 4)
                                sp.wait_ge(x1_stored[1], 16 * (p.n - X1_FIRST))
                            sp.dma_start((za, zb)[k][:], x_rows[:, :, bass.ds(p.cols[k][0] + p.cols[k][1] * p.i, GRP)]) \
                                .then_inc(res_loaded[k], 16)
                    if p.n0 == X1_FIRST and b in (10, 28):
                        k = (b - 10) // 18
                        if k == 0:
                            sp.wait_ge(x_filled, p.x0)
                        else:
                            sp.wait_ge(gt_filled, 8 * HB)
                        sp.dma_start((za, zb)[k][:], x_rows[:, :, k * GRP:(k + 1) * GRP]).then_inc(res_loaded[k], 16)
                    if p.side == "k" and p.batch0 is None and p.n0 == ATTN_PAIRS[8].n0 - 1 and b == 10:
                        sp.wait_ge(maxima, maxima_after("B", 2 * A_HEADS - 1))
                        sp.dma_start(dist[:], neg_dist_c).then_inc(dist_loaded, 16)
                    if p.n0 == X2_FIRST and b >= 8 and b % 2 == 0:
                        if b == 8:
                            sp.wait_ge(block_done, X2_FIRST * NB)
                            sp.wait_ge(x1_stored[0], 16 * 4)
                            sp.wait_ge(x1_stored[1], 16 * 4)
                        m = (b - 8) // 2
                        if m < 4:
                            cols = slice(m * 2 * GRP, (m + 1) * 2 * GRP)
                            sp.dma_start(x_fin[:, :, cols], x1_rows[:, :, cols]).then_inc(fin_loaded, 16)
                        elif m < 8:
                            cols = slice((m - 4) * 2 * GRP, (m - 3) * 2 * GRP)
                            sp.dma_start(fin_w[:, cols], final_w[cols].partition_broadcast(P)).then_inc(fin_loaded, 16)

            walk(sp, body)
            for k, (first, last_col) in enumerate(OUT_PIECES):
                cols = slice(first, last_col)
                sp.wait_ge(scaled, k + 1)
                sp.dma_start(out_rows[:, 0, cols], x_fin[:, 0, cols]).then_inc(out_stored, 16)
                sp.wait_ge(scaled_act, k + 1)
                sp.dma_start(out_rows[:, 1, cols], x_fin[:, 1, cols]).then_inc(out_stored, 16)
            sp.wait_ge(out_stored, 16 * TT * len(OUT_PIECES))

        @block.gpsimd
        def _(pool):
            nc.gpsimd.memset(minus_half[:], -0.5).then_inc(minus_half_set, 1)
            pool.wait_ge(minus_half_set, 1)
            for n, (dst, cols) in enumerate([(rms, TT)] + [(head_rms, TT * HB)] * 5 + [(rms, TT)] * 2):
                pool.wait_ge(var_ready, n + 1)
                nc.gpsimd.tensor_tensor(dst[:, 0:cols], var[:, 0:cols], minus_half[:, 0:cols], ALU.pow) \
                    .then_inc(pow_done, 1)

        @block.scalar
        def _(act):
            def split_hi_first(n):
                act.wait_ge(raw_loaded[n], 16)
                nc.scalar.activation(w_hi[:, n], raw[:, n], ACT.Copy).then_inc(hi_ready, 1)

            def first_x(m):
                act.wait_ge(first_filled, m + 1)
                for j in range(2):
                    k = 2 * m + j
                    last = nc.scalar.activation(h_hi[:, k], first_ps[m % 4][:, j], ACT.Copy, scale=norm_w[:, 0, k:k + 1])
                last.then_inc(first_hi, 1)

            def split_hi_at(p, b):
                m = ahead(p, b)
                if m is None:
                    return
                n, slot = m
                if not (isinstance(n, int) and n < RING):
                    act.wait_ge(block_done, n - RING + 1)
                act.wait_ge(raw_loaded[slot], 16 * (p.n * (NB // RING) + (b + AHEAD) // RING + 1))
                nc.scalar.activation(w_hi[:, slot], raw[:, slot], ACT.Copy).then_inc(hi_ready, 1)
                act.wait_ge(hi_ready, n + 1)

            def drain(p, g, out, n):
                act.wait_ge(block_done, n * NB + (DONE0 if g == 0 else NB))
                for t in range(TT):
                    src, scale = proj[g][t], rms[:, t:t + 1]
                    if (g, out) in ((0, "vg"), (1, "kv")):
                        nc.scalar.activation(v_hi[:, t], src[:], ACT.Copy, scale=scale).then_inc(v_hi_ready, 1)
                    elif g == 1 and out in ("qg", "vg"):
                        nc.scalar.activation(zb[:, t], src[:], ACT.Silu, scale=scale).then_inc(drained[g], 1)
                    else:
                        nc.scalar.activation((za, zb)[g][:, t], src[:], ACT.Copy, scale=scale).then_inc(drained[g], 1)

            act.wait_ge(minus_half_set, 1)
            nc.scalar.activation(warm[:], minus_half[:, 0:1], ACT.Copy)
            act.wait_ge(norm_loaded, 16)
            for n in range(FIRST_AHEAD):
                first_x(n)
                if n < AHEAD:
                    split_hi_first(n)

            def body(p):
                for b in range(NB):
                    split_hi_at(p, b)
                    if p.n0 == 0 and b + FIRST_AHEAD < KC // 2:
                        first_x(b + FIRST_AHEAD)
                    if b == 0 and p.before not in (None, "x1", "x2"):
                        drain(p, 1, p.before, p.n - 1)
                    if b == DRAIN0 and p.out not in ("x1", "x2"):
                        if p.n0 == 0:
                            act.wait_ge(pow_done, 1)
                        if p.n0 == X1_FIRST + 4:
                            act.wait_ge(pow_done, 7)
                            act.wait_ge(x1_stored[0], 16 * 4)
                            act.wait_ge(x1_stored[1], 16 * 4)
                            act.wait_ge(summed, 4 * 4 + 1)
                        drain(p, 0, p.out, p.n)
                    for k, dst, m in rounds_at(p, b):
                        act.wait_ge(x_filled, p.x0 + k + 1)
                        dst = {"q": qT_hi, "k": kT_hi}[dst]
                        nc.scalar.activation(dst[:, 2 * m:2 * m + 2], x_ps[:], ACT.Copy).then_inc(x_hi, 1)
                    if p.side == "h" and b in H_STEPS:
                        m = H_STEPS.index(b)
                        act.wait_ge(x_filled, p.x0 + m + 1)
                        for j in range(2):
                            k = (p.x_batch0 + p.i) * 8 + 2 * m + j
                            last = nc.scalar.activation(h_hi[:, bass.ds(k, 1)].rearrange("p a n -> p (a n)"), x_ps[:, j],
                                                        ACT.Copy, scale=norm_w[:, 1, bass.ds(k, 1)])
                        last.then_inc(x_hi, 1)
                    if p.side in ("A", "B", "C"):
                        attend(p, b)

            def attend(p, b):
                i = head_at(p, b, TO_PROBS)
                if i is not None:
                    h = p.batch * HB + i
                    act.wait_ge(maxima, maxima_after(p.side, h))
                    for t in range(TT):
                        scale = {"A": q_scale[:, t * HB + i:t * HB + i + 1], "B": 1.0, "C": SCALE}[p.side]
                        last = nc.scalar.activation(probs[:, t], sc_ps[:, t], ACT.Exp, bias=exp_bias[:, t:t + 1],
                                                    scale=scale, accum_out=sums[:, t:t + 1])
                    if p.side == "C":
                        last = nc.scalar.activation(sink_term[:], exp_bias[:], ACT.Exp, bias=sink[:, bass.ds(h - 32, 1)])
                    last.then_inc(probs_ready, 1)
                if head_at(p, b, TO_PROBS) == 0 and p.side in ("A", "C"):
                    act.wait_ge(drained[1], 2 * p.n)
                    if p.batch0 > 0:
                        act.wait_ge(pv_done, p.batch * HB)
                    cols = bass.ds(kv_head(p) * HD, HD)
                    nc.scalar.activation(pick_hi[:], v_hi[:, :, cols].bitcast(F32), ACT.Copy).then_inc(v_picked, 1)
                    nc.scalar.activation(pick_lo[:], v_lo[:, :, cols].bitcast(F32), ACT.Copy).then_inc(v_picked, 1)
                i = head_at(p, b, TO_PT)
                if i is not None:
                    h = p.batch * HB + i
                    act.wait_ge(pt_filled, h + 1)
                    nc.scalar.activation(probsT_hi[:], tr_ps[:], ACT.Copy).then_inc(pt_hi_ready, 1)
                i = head_at(p, b, TO_GT)
                if i is not None:
                    h = p.batch * HB + i
                    act.wait_ge(gt_filled, h + 1)
                    if p.batch0 > 0 or i > 0:
                        act.wait_ge(y_split, h)
                    nc.scalar.activation(y[:], o_ps[:, 1], ACT.Copy).then_inc(gt_ready, 1)
                i = head_at(p, b, TO_Y)
                if i is not None:
                    h = p.batch * HB + i
                    row = (p.batch - (8 if p.side == "C" else 0)) * HB + i
                    act.wait_ge(y_made, h + 1)
                    nc.scalar.activation(y_hi[:, bass.ds(row, 1)].rearrange("p a n -> p (a n)"), y[:], ACT.Copy) \
                        .then_inc(y_hi_ready, 1)

            walk(act, body)
            act.wait_ge(pow_done, 8)
            act.wait_ge(x2_steps, 4 * 7 + 3)
            for first, last_col in OUT_PIECES:
                cols = slice(first, last_col)
                nc.scalar.activation(x_fin[:, 1, cols], x_fin[:, 1, cols], ACT.Copy, scale=rms[:, 1:2]) \
                    .then_inc(scaled_act, 1)

        @block.vector
        def _(dve):
            def split_lo(p, b):
                m = ahead(p, b)
                if m is None:
                    return
                n, slot = m
                dve.wait_ge(hi_ready, n + 1)
                nc.vector.tensor_tensor(w_lo[:, slot], raw[:, slot], w_hi[:, slot].bitcast(F32), ALU.subtract) \
                    .then_inc(lo_ready, 1)
                dve.wait_ge(lo_ready, n + 1)

            def first_x(m):
                dve.wait_ge(first_hi, m + 1)
                for j in range(2):
                    k = 2 * m + j
                    last = nc.vector.scalar_tensor_tensor(h_lo[:, k], first_ps[m % 4][:, j], norm_w[:, 0, k:k + 1],
                                                          h_hi[:, k].bitcast(F32), ALU.mult, ALU.subtract)
                last.then_inc(first_split, 1)

            def drain_v(p, g, n):
                for t in range(TT):
                    dve.wait_ge(v_hi_ready, TT * p.v + t + 1)
                    nc.vector.scalar_tensor_tensor(v_lo[:, t], proj[g][t][:], rms[:, t:t + 1], v_hi[:, t].bitcast(F32),
                                                   ALU.mult, ALU.subtract).then_inc(drained[g], 1)

            dve.wait_ge(norm_loaded, 16)
            for n in range(FIRST_AHEAD):
                first_x(n)
                if n < AHEAD:
                    dve.wait_ge(hi_ready, n + 1)
                    nc.vector.tensor_tensor(w_lo[:, n], raw[:, n], w_hi[:, n].bitcast(F32), ALU.subtract) \
                        .then_inc(lo_ready, 1)

            def first_squares(b):
                if 14 <= b < 22:
                    m = b - 14
                    cols = slice(m * GRP, (m + 1) * GRP)
                    for t in range(TT):
                        last = nc.vector.tensor_tensor_reduce(swap[:, t], x_in[:, t, cols], x_in[:, t, cols], 1.0, 0.0,
                                                              ALU.mult, ALU.add, sq_cols[:, t, m:m + 1])
                    last.then_inc(squared, 1)
                if b == 22:
                    dve.wait_ge(squared, 8)
                    nc.vector.tensor_reduce(sq_sum[:], sq_cols[:], AX_X, ALU.add).then_inc(squared, 1)
                    dve.wait_ge(squared, 9)
                    nc.vector.tensor_scalar(var[:, 0:TT], sq_sum[:], 1.0 / DM, EPS, ALU.mult, ALU.add).then_inc(var_ready, 1)
                if b == 24:
                    dve.wait_ge(tables_loaded, 16 * 8)
                    nc.vector.tensor_scalar(neg_sink[:], sink[:], -1.0, None, ALU.mult)
                    nc.vector.memset(sq_sum[:], 0.0).then_inc(summed, 1)
                if b == 25:
                    halves = lambda ap: ap.rearrange("p (h q e) -> p h q e", h=2, q=2)
                    for cos, sin, w in ((cos_q, sin_q, norm_bc[:, 0]), (cos_k, sin_k, norm_bc[:, 1])):
                        for t in range(TT):
                            nc.vector.tensor_tensor(cos[:, t], cos[:, t], w, ALU.mult).then_inc(tables_made, 1)
                            for q in range(2):
                                s = halves(sin[:, t])[:, :, q]
                                last = nc.vector.tensor_tensor(s, s, halves(w)[:, :, 1 - q], ALU.mult)
                            last.then_inc(tables_made, 1)

            def rope(b, cos, sin, k, for_k):
                s = k * ROPE_STEPS
                heads = za[:].rearrange("p t (h d) -> p (t h) d", d=HD)
                if b == 0:
                    dve.wait_ge(tables_made, TABLE_STEPS)
                    nc.vector.tensor_tensor(swap[:], za[:], za[:], ALU.mult).then_inc(roped, 1)
                    dve.wait_ge(roped, s + 1)
                    nc.vector.tensor_reduce(q_scale[:], swap[:].rearrange("p t (h d) -> p (t h) d", d=HD), AX_X, ALU.add) \
                        .then_inc(roped, 1)
                    dve.wait_ge(roped, s + 2)
                    nc.vector.tensor_scalar(var[:], q_scale[:], 1.0 / HD, EPS, ALU.mult, ALU.add).then_inc(var_ready, 1)
                if b == 1:
                    quarters = lambda ap: ap.rearrange("p (h f q e) -> p (h f) q e", h=HB, f=2, q=2)
                    for t in range(TT):
                        for q in range(2):
                            sines = sin[:, t].rearrange("p (f q e) -> p f q e", f=2, q=2)[:, :, q]
                            nc.vector.tensor_tensor(
                                swap[:, t].rearrange("p (h f q e) -> p h f q e", h=HB, f=2, q=2)[:, :, :, q],
                                za[:, t].rearrange("p (h f q e) -> p h f q e", h=HB, f=2, q=2)[:, :, :, 1 - q],
                                sines.unsqueeze(1).to_broadcast([P, HB, 2, HD // 4]), ALU.mult).then_inc(roped, 1)
                if b == 2:
                    dve.wait_ge(roped, s + 6)
                    for t in range(TT):
                        last = nc.vector.tensor_tensor(za[:, t].rearrange("p (h d) -> p h d", h=HB),
                                                       za[:, t].rearrange("p (h d) -> p h d", h=HB),
                                                       cos[:, t].unsqueeze(1).to_broadcast([P, HB, HD]), ALU.mult)
                    last.then_inc(roped, 1)
                    dve.wait_ge(roped, s + 7)
                    nc.vector.tensor_tensor(za[:], za[:], swap[:], ALU.add).then_inc(roped, 1)
                    dve.wait_ge(pow_done, k + 2)
                    dve.wait_ge(roped, s + 8)
                    if for_k:
                        nc.vector.tensor_tensor(heads, heads, head_rms[:].unsqueeze(2).to_broadcast([P, TT * HB, HD]),
                                                ALU.mult).then_inc(roped, 1)
                    else:
                        nc.vector.tensor_scalar(q_scale[:], head_rms[:], SCALE, None, ALU.mult).then_inc(roped, 1)

            def attend(p, b):
                i = head_at(p, b, TO_PROBS)
                if i is not None:
                    h = p.batch * HB + i
                    m = maxima_after(p.side, h - 1)
                    dve.wait_ge(scored, h + 1)
                    if p.side == "B":
                        if i < 2:
                            dve.wait_ge(bias_loaded[i], 32 * (p.batch - 4) + 16)
                        else:
                            dve.wait_ge(bias_loaded[i - 2], 32 * (p.batch - 4) + 32)
                        nc.vector.scalar_tensor_tensor(sc_ps[:], sc_ps[:], SCALE, bias[:, i % 2], ALU.mult, ALU.add) \
                            .then_inc(maxima, 1)
                        dve.wait_ge(maxima, m + 1)
                    if p.side == "C":
                        nc.vector.scalar_tensor_tensor(sc_ps[:], dist[:], slope[:, bass.ds(h - 32, 1)], sc_ps[:],
                                                       ALU.mult, ALU.add).then_inc(maxima, 1)
                        dve.wait_ge(maxima, m + 1)
                    dst = exp_bias if p.side == "B" else neg_max
                    nc.vector.tensor_reduce(dst[:], sc_ps[:], AX_X, ALU.max, negate=True).then_inc(maxima, 1)
                    if p.side == "A":
                        dve.wait_ge(maxima, m + 1)
                        scales = q_scale[:].rearrange("p (t h) -> p t h", t=TT)[:, :, i]
                        nc.vector.tensor_tensor(exp_bias[:], neg_max[:], scales, ALU.mult).then_inc(maxima, 1)
                    if p.side == "C":
                        dve.wait_ge(maxima, m + 2)
                        nc.vector.tensor_scalar(exp_bias[:], neg_max[:], SCALE, neg_sink[:, bass.ds(h - 32, 1)],
                                                ALU.mult, ALU.min).then_inc(maxima, 1)
                i = head_at(p, b, TO_PT)
                if i is not None:
                    h = p.batch * HB + i
                    dve.wait_ge(probs_ready, h + 1)
                    if p.side == "C":
                        nc.vector.tensor_tensor(total[:], sums[:], sink_term[:], ALU.add).then_inc(inverses, 1)
                        dve.wait_ge(inverses, inverses_after("C", h) - 1)
                    nc.vector.reciprocal(inv_sum[:], (total if p.side == "C" else sums)[:]).then_inc(inverses, 1)
                    dve.wait_ge(inverses, inverses_after(p.side, h))
                    if i == 0:
                        dve.wait_ge(drained[1], 2 * p.n)
                    for t in range(TT):
                        z = zb[:, t, i * HD:(i + 1) * HD]
                        last = nc.vector.tensor_scalar(z, z, inv_sum[:, t:t + 1], None, ALU.mult)
                    last.then_inc(gate_scaled, 1)
                    dve.wait_ge(pt_hi_ready, h + 1)
                    nc.vector.tensor_tensor(probsT_lo[:], tr_ps[:], probsT_hi[:].bitcast(F32), ALU.subtract) \
                        .then_inc(pt_split, 1)
                i = head_at(p, b, TO_REST)
                if i is not None:
                    h = p.batch * HB + i
                    row = (p.batch - (8 if p.side == "C" else 0)) * HB + i
                    dve.wait_ge(y_hi_ready, h + 1)
                    nc.vector.tensor_tensor(y_lo[:, bass.ds(row, 1)].rearrange("p a n -> p (a n)"), y[:],
                                            y_hi[:, bass.ds(row, 1)].rearrange("p a n -> p (a n)").bitcast(F32),
                                            ALU.subtract).then_inc(y_split, 1)
                i = head_at(p, b, TO_Y)
                if i is not None:
                    h = p.batch * HB + i
                    dve.wait_ge(pv_done, h + 1)
                    nc.vector.tensor_tensor(y[:], o_ps[:, 0], y[:], ALU.mult).then_inc(y_made, 1)

            def add_x1(g, n):
                dve.wait_ge(block_done, n * NB + (DONE0 if g == 0 else NB))
                dve.wait_ge(res_loaded[g], 16 * (n - X1_FIRST + 1))
                for t in range(TT):
                    z = (za, zb)[g]
                    nc.vector.tensor_tensor(z[:, t], proj[g][t][:], z[:, t], ALU.add).then_inc(drained[g], 1)

            def square_x1(p, g):
                z = (za, zb)[g]
                s = 4 * (p.n - 1 - X1_FIRST) + 2 * g + 1
                dve.wait_ge(drained[g], 2 * p.n)
                dve.wait_ge(summed, s)
                for t in range(TT):
                    last = nc.vector.tensor_tensor_reduce(swap[:, t], z[:, t], z[:, t], 1.0, 0.0, ALU.mult, ALU.add,
                                                          sq_part[:, t:t + 1])
                last.then_inc(summed, 1)
                dve.wait_ge(summed, s + 1)
                nc.vector.tensor_tensor(sq_sum[:], sq_sum[:], sq_part[:], ALU.add).then_inc(summed, 1)

            def add_x2(p, g, n, groups):
                s = 4 * (2 * (n - X2_FIRST) + g)
                first = groups * GRP
                cols = bass.ds(first, GRP)
                dve.wait_ge(block_done, n * NB + (DONE0 if g == 0 else NB))
                if not isinstance(s, int) or s:
                    dve.wait_ge(x2_steps, s)
                for t in range(TT):
                    nc.vector.tensor_tensor(za[:, t], proj[g][t][:], x_fin[:, t, cols], ALU.add).then_inc(drained[g], 1)
                dve.wait_ge(drained[g], 2 * (n + 1))
                for t in range(TT):
                    last = nc.vector.tensor_tensor_reduce(swap[:, t], za[:, t], za[:, t], 1.0, 0.0, ALU.mult, ALU.add,
                                                          sq_part[:, t:t + 1])
                last.then_inc(x2_steps, 1)
                dve.wait_ge(x2_steps, s + 1)
                nc.vector.tensor_tensor(sq_sum[:], sq_sum[:], sq_part[:], ALU.add).then_inc(x2_steps, 1)
                for t in range(TT):
                    nc.vector.tensor_tensor(x_fin[:, t, cols], za[:, t], fin_w[:, cols], ALU.mult).then_inc(x2_steps, 1)

            def body(p):
                for b in range(NB):
                    split_lo(p, b)
                    if p.n0 == 0:
                        if b + FIRST_AHEAD < KC // 2:
                            first_x(b + FIRST_AHEAD)
                        first_squares(b)
                    if b == 0 and p.before == "kv":
                        drain_v(p, 1, p.n - 1)
                    if b == DRAIN0 and p.out == "vg":
                        drain_v(p, 0, p.n)
                    for k, dst, m in rounds_at(p, b):
                        dve.wait_ge(x_hi, p.x0 + k + 1)
                        hi, lo = {"q": (qT_hi, qT_lo), "k": (kT_hi, kT_lo)}[dst]
                        nc.vector.tensor_tensor(lo[:, 2 * m:2 * m + 2], x_ps[:], hi[:, 2 * m:2 * m + 2].bitcast(F32),
                                                ALU.subtract).then_inc(x_drained, 1)
                    if b == 0 and p.before == "x1":
                        add_x1(1, p.n - 1)
                    if b == 0 and p.before == "x2":
                        add_x2(p, 1, p.n - 1, (p.n - 1 - X2_FIRST) * 2 + 1)
                    if b == DRAIN0 and p.out == "x1":
                        add_x1(0, p.n)
                    if b == DRAIN0 and p.out == "x2":
                        if p.n0 == X2_FIRST:
                            dve.wait_ge(fin_loaded, 16 * 8)
                        add_x2(p, 0, p.n, (p.n - X2_FIRST) * 2)
                    if p.side == "k_norm":
                        if b == 0:
                            dve.wait_ge(drained[0], 2 * p.n)
                        rope(b, cos_k, sin_k, 0, True)
                    if p.side == "A":
                        if b == 0:
                            dve.wait_ge(drained[0], 2 * p.n)
                        rope(b, cos_q, sin_q, p.batch + 1, False)
                    if p.side == "h":
                        if b in (1, 3):
                            square_x1(p, (b - 1) // 2)
                        if b in H_STEPS:
                            m = H_STEPS.index(b)
                            dve.wait_ge(x_hi, p.x0 + m + 1)
                            for j in range(2):
                                k = (p.x_batch0 + p.i) * 8 + 2 * m + j
                                last = nc.vector.scalar_tensor_tensor(
                                    h_lo[:, bass.ds(k, 1)].rearrange("p a n -> p (a n)"), x_ps[:, j],
                                    norm_w[:, 1, bass.ds(k, 1)],
                                    h_hi[:, bass.ds(k, 1)].rearrange("p a n -> p (a n)").bitcast(F32),
                                    ALU.mult, ALU.subtract)
                            last.then_inc(x_drained, 1)
                        if p.out == "kv" and b == 10:
                            dve.wait_ge(summed, 4 * 4 + 1)
                            nc.vector.tensor_scalar(var[:, 0:TT], sq_sum[:], 1.0 / DM, EPS, ALU.mult, ALU.add) \
                                .then_inc(var_ready, 1)
                        if p.out == "kv" and b == 12:
                            nc.vector.memset(sq_sum[:], 0.0).then_inc(summed, 1)
                    if p.side in ("A", "B", "C"):
                        if p.side == "C" and p.batch0 == 8 and b == 0:
                            dve.wait_ge(dist_loaded, 16)
                        attend(p, b)

            walk(dve, body)
            n, steps, cols = PAIRS_ALL - 1, 4 * 7, slice(7 * GRP, 8 * GRP)
            dve.wait_ge(x2_steps, steps)
            for t in range(TT):
                dve.wait_ge(last_tile, t + 1)
                nc.vector.tensor_tensor(za[:, t], proj[1][t][:], x_fin[:, t, cols], ALU.add).then_inc(drained[1], 1)
                dve.wait_ge(drained[1], 2 * n + t + 1)
                last = nc.vector.tensor_tensor_reduce(swap[:, t], za[:, t], za[:, t], 1.0, 0.0, ALU.mult, ALU.add,
                                                      sq_part[:, t:t + 1])
            last.then_inc(x2_steps, 1)
            dve.wait_ge(x2_steps, steps + 1)
            nc.vector.tensor_tensor(sq_sum[:], sq_sum[:], sq_part[:], ALU.add).then_inc(x2_steps, 1)
            dve.wait_ge(x2_steps, steps + 2)
            nc.vector.tensor_scalar(var[:, 0:TT], sq_sum[:], 1.0 / DM, EPS, ALU.mult, ALU.add).then_inc(var_ready, 1)
            nc.vector.tensor_tensor(x_fin[:, 1, cols], za[:, 1], fin_w[:, cols], ALU.mult).then_inc(x2_steps, 1)
            dve.wait_ge(pow_done, 8)
            for first, last_col in OUT_PIECES:
                piece = slice(first, min(last_col, cols.start))
                work = nc.vector.tensor_scalar(x_fin[:, 0, piece], x_fin[:, 0, piece], rms[:, 0:1], None, ALU.mult)
                if last_col == DM:
                    work = nc.vector.scalar_tensor_tensor(x_fin[:, 0, cols], za[:, 0], rms[:, 0:1], fin_w[:, cols],
                                                          ALU.mult, ALU.mult)
                work.then_inc(scaled, 1)

        @block.tensor
        def _(pe):
            def first_x(m):
                if m % 2 == 0:
                    pe.wait_ge(x_loaded[m // 2], 16)
                if m >= 4:
                    pe.wait_ge(first_split, m - 3)
                for j in range(2):
                    for t in range(TT):
                        k = 2 * m + j
                        last = nc.tensor.transpose(first_ps[m % 4][:, j, t * P:(t + 1) * P],
                                                   x_in[:, t, k * P:(k + 1) * P], ident[:])
                last.then_inc(first_filled, 1)

            def three_passes(dst, hi, lo, r_hi, r_lo, start, stop):
                nc.tensor.matmul(dst, hi, r_hi, start=start, stop=False)
                nc.tensor.matmul(dst, hi, r_lo, start=False, stop=False)
                return nc.tensor.matmul(dst, lo, r_hi, start=False, stop=stop)

            pe.wait_ge(ident_loaded, 16)
            for m in range(FIRST_AHEAD):
                first_x(m)

            def product(p, b):
                g, c = BLOCKS[b]
                hi, lo = (y_hi, y_lo) if p.w in ("out_ab", "out_c") else (h_hi, h_lo)
                slot = b % RING
                pe.wait_ge(lo_ready, p.n * NB + b + 1)
                if c == 0 and p.n0 > 0:
                    pe.wait_ge(drained[g], 2 * p.n)
                if p.n0 == 0 and g == 0:
                    pe.wait_ge(first_split, c + 1)
                if p.n0 == X1_FIRST + 4 and g == 0:
                    pe.wait_ge(x_drained, H_FIRST_X + c + 1)
                if p.n0 in (X1_FIRST, X2_FIRST) and g == 0:
                    first = 0 if p.n0 == X1_FIRST else 32
                    pe.wait_ge(y_split, first + 2 * c + 2)
                by_tile = p.last and b == NB - 1
                for j, t in [(j, t) for t in range(TT) for j in range(2)] if by_tile else \
                        [(j, t) for j in range(2) for t in range(TT)]:
                    k = 2 * c + j
                    toks = slice(t * P, (t + 1) * P)
                    last = three_passes(proj[g][t][:], hi[:, k, toks], lo[:, k, toks], w_hi[:, slot, j],
                                        w_lo[:, slot, j], k == 0, k == KC - 1)
                    if by_tile and j == 1:
                        last.then_inc(last_tile, 1)
                if not by_tile:
                    last.then_inc(block_done, 1)

            def heads_round(p, k, src, i):
                if not (isinstance(p.x0, int) and p.x0 + k == 0):
                    pe.wait_ge(x_drained, p.x0 + k)
                for j in range(2):
                    for t in range(TT):
                        d = (2 * i + j) * HD
                        last = nc.tensor.transpose(x_ps[:, j, t * P:(t + 1) * P], src[:, t, d:d + HD], ident[:])
                last.then_inc(x_filled, 1)

            def attend(p, b):
                kv = kv_head(p)
                i = head_at(p, b, 0)
                if i is not None:
                    h = p.batch * HB + i
                    if i == 0:
                        pe.wait_ge(x_drained, p.x0 + p.x_uses)
                    if p.batch0 > 0 or i > 0:
                        pe.wait_ge(probs_ready, h)
                    k_hi, k_lo = (k[:, i] if p.side == "B" else k[:, bass.ds(kv, 1)].rearrange("p a n -> p (a n)")
                                  for k in (kT_hi, kT_lo))
                    for t in range(TT):
                        toks = slice(t * P, (t + 1) * P)
                        last = three_passes(sc_ps[:, t], qT_hi[:, i, toks], qT_lo[:, i, toks], k_hi, k_lo, True, True)
                    last.then_inc(scored, 1)
                i = head_at(p, b, TO_PT)
                if i is not None:
                    h = p.batch * HB + i
                    pe.wait_ge(probs_ready, h + 1)
                    for kt in range(TT):
                        for t in range(TT):
                            last = nc.tensor.transpose(tr_ps[:, kt, t * P:(t + 1) * P],
                                                       probs[:, t, kt * P:(kt + 1) * P], ident[:])
                    last.then_inc(pt_filled, 1)
                i = head_at(p, b, TO_GT)
                if i is not None:
                    h = p.batch * HB + i
                    pe.wait_ge(gate_scaled, h + 1)
                    if p.batch0 > 0 or i > 0:
                        pe.wait_ge(y_made, h)
                    for t in range(TT):
                        last = nc.tensor.transpose(o_ps[:, 1, t * P:(t + 1) * P], zb[:, t, i * HD:(i + 1) * HD], ident[:])
                    last.then_inc(gt_filled, 1)
                i = head_at(p, b, TO_PV)
                if i is not None:
                    h = p.batch * HB + i
                    pe.wait_ge(pt_split, h + 1)
                    pe.wait_ge(gt_ready, h + 1)
                    if p.side == "B":
                        cols, hi, lo = slice(i * HD, (i + 1) * HD), v_hi, v_lo
                    else:
                        cols, hi, lo = slice(0, HD), pick_hi, pick_lo
                        if i == 0:
                            pe.wait_ge(v_picked, 2 * (p.batch + 1 - (0 if p.side == "A" else 4)))
                    for kt in range(TT):
                        last = three_passes(o_ps[:, 0], hi[:, kt, cols], lo[:, kt, cols], probsT_hi[:, kt],
                                            probsT_lo[:, kt], kt == 0, kt == TT - 1)
                    last.then_inc(pv_done, 1)

            def body(p):
                for b in range(NB):
                    for k, dst, m in rounds_at(p, b):
                        if p.side in ("A", "k_norm"):
                            if k == 0:
                                pe.wait_ge(roped, ROPE_STEPS * (1 if p.side == "k_norm" else p.batch + 2))
                        elif m == 0:
                            pe.wait_ge(drained[k // 2], 2 * p.n)
                        heads_round(p, k, zb if p.side == "qk" and dst == "k" else za, m)
                    if p.side == "h" and b in H_STEPS:
                        m = H_STEPS.index(b)
                        if m in (0, 2):
                            pe.wait_ge(drained[m // 2], 2 * p.n)
                        heads_round(p, m, (za, zb)[m // 2], m % 2)
                    if p.side in ("A", "B", "C"):
                        attend(p, b)
                    product(p, b)
                    if p.n0 == 0 and b + FIRST_AHEAD < KC // 2:
                        first_x(b + FIRST_AHEAD)

            walk(pe, body)


def constants():
    pos = np.arange(SEQ)
    half, quarter = HD // 2, HD // 4
    inv = np.exp(-np.log(10000.0) * np.arange(0, half, 2, dtype=np.float64) / half)
    cos = np.zeros((SEQ, HD))
    sin = np.zeros((SEQ, HD))
    for h, coord in enumerate((pos // GRID_W, pos % GRID_W)):
        ang = coord.astype(np.float32)[:, None] * inv.astype(np.float32)[None, :]
        lo = h * half
        cos[:, lo:lo + quarter] = cos[:, lo + quarter:lo + half] = np.cos(ang)
        sin[:, lo:lo + quarter] = -np.sin(ang)
        sin[:, lo + quarter:lo + half] = np.sin(ang)
    tiles = lambda a: np.ascontiguousarray(a.reshape(TT, P, -1).transpose(1, 0, 2).astype(np.float32))
    dist = np.abs(pos[:, None] - pos[None, :])
    neg_dist = np.where(dist <= C_WINDOW, -dist.astype(np.float64), NEG)
    slopes = np.exp2(-8.0 * np.arange(1, C_HEADS + 1) / C_HEADS) / SCALE
    return {
        "ident_c": np.eye(P, dtype=np.float32),
        "cos_c": tiles(cos),
        "sin_c": tiles(sin),
        "neg_dist_c": tiles(neg_dist),
        "slopes_c": np.broadcast_to(slopes.astype(np.float32), (P, C_HEADS)).copy(),
    }


def bias_layout(rpb):
    pos = np.arange(SEQ)
    r, c = pos // GRID_W, pos % GRID_W
    wr = min(NA_ROWS_MAX, ROWS)
    rs = np.clip(r - wr // 2, 0, ROWS - wr)
    cs = np.clip(c - NA_COLS // 2, 0, GRID_W - NA_COLS)
    inside = ((r[None, :] >= rs[:, None]) & (r[None, :] < rs[:, None] + wr)
              & (c[None, :] >= cs[:, None]) & (c[None, :] < cs[:, None] + NA_COLS))
    dr = np.clip(r[None, :] - r[:, None] + NA_ROWS_MAX - 1, 0, 2 * NA_ROWS_MAX - 2)
    dc = np.clip(c[None, :] - c[:, None] + NA_COLS - 1, 0, 2 * NA_COLS - 2)
    return np.where(inside[None], rpb[:, dr, dc], np.float32(NEG))


def kernel(**inputs):
    import concourse.bacc as _bacc
    from concourse.bass_utils import run_bass_kernel_spmd as _run

    a = {k: np.asarray(val) for k, val in inputs.items()}
    arrays = {
        "x": a["x"][0],
        "w_in_ab": a["w_in_ab"][0],
        "w_out_ab": a["w_out_ab"][0],
        "w_in_c": a["w_in_c"][0],
        "w_out_c": a["w_out_c"][0],
        "norm_cols": a["norm_w"].reshape(2, KC, P).transpose(2, 0, 1),
        "q_norm": a["q_norm_a"][0],
        "k_norm": a["k_norm_a"][0],
        "final_w": a["final_norm_w"],
        "bias_b": bias_layout(a["rpb_b"][0]),
        "sinks": a["sink_c"][0],
    }
    arrays.update(constants())
    nc = _bacc.Bacc("TRN2", target_bir_lowering=False, num_devices=1, dynamic_dma_scratch_size=SWDGE_BYTES)
    ins, aps = {}, []
    for name, val in arrays.items():
        ins[f"in_{name}"] = np.ascontiguousarray(val)
        aps.append(nc.dram_tensor(f"in_{name}", val.shape, mybir.dt.from_np(val.dtype), kind="ExternalInput").ap())
    out = nc.dram_tensor("out_0", (SEQ, DM), F32, kind="ExternalOutput").ap()
    build(nc, *aps, out)
    r = _run(nc, [ins], core_ids=[0])
    return r.results[0]["out_0"].reshape(1, SEQ, DM)
```
